# Optimizing a Trainium2 kernel written in Bass

```python
import math
import jax, jax.numpy as jnp
from jax import lax
import numpy as np

D_MODEL = 1024
BATCH = 1
SEQ = 256
DEPTH = 1
DEC_BATCH = 1
DEC_SEQ = 64
PAST_LEN = 512

CHUNK = 64
EPS = 1e-6
D_S5 = 512
S5_GROUP = 16
S5_GROUPS = D_S5 // S5_GROUP
S5_STATE = 64
ML_HEADS = 4
ML_HEAD_DIM = 128
D_ML = ML_HEADS * ML_HEAD_DIM
N_EXPERTS = 32
TOP_K = 4
D_FF = 1024
SWIGLU_LIMIT = 7.0
SWIGLU_ALPHA = 1.702
MOE_BLOCK = 128
D_IN = D_S5 + 4 * D_ML + 2 * ML_HEADS + 2 * D_MODEL

kernel_name = 'hybrid_s5_mlstm_moe_stream_step'

def rmsnorm(x, w):
    xf = x.astype(jnp.float32)
    xf = xf * lax.rsqrt(jnp.mean(xf * xf, axis=-1, keepdims=True) + EPS)
    return (xf * w.astype(jnp.float32)).astype(x.dtype)

def _complex_affine_combine(e1, e2):
    a1r, a1i, b1r, b1i = e1
    a2r, a2i, b2r, b2i = e2
    return (a2r * a1r - a2i * a1i,
            a2r * a1i + a2i * a1r,
            a2r * b1r - a2i * b1i + b2r,
            a2r * b1i + a2i * b1r + b2i)

def s5_scan(u, h0_re, h0_im, a_re, a_im, log_dt, b_re, b_im, c_re, c_im, d_skip):
    f32 = jnp.float32
    bsz, L, _ = u.shape
    uf = u.astype(f32).reshape(bsz, L, S5_GROUPS, S5_GROUP)
    ar = a_re.astype(f32)
    ai = a_im.astype(f32)
    dt = jnp.exp(log_dt.astype(f32))[:, None]
    mag = jnp.exp(dt * ar)
    abar_re = mag * jnp.cos(dt * ai)
    abar_im = mag * jnp.sin(dt * ai)
    den = ar * ar + ai * ai
    fr = ((abar_re - 1.0) * ar + abar_im * ai) / den
    fi = (abar_im * ar - (abar_re - 1.0) * ai) / den
    br = b_re.astype(f32)
    bi = b_im.astype(f32)
    bbar_re = fr[..., None] * br - fi[..., None] * bi
    bbar_im = fr[..., None] * bi + fi[..., None] * br
    bu_re = jnp.einsum('blgc,gpc->blgp', uf, bbar_re)
    bu_im = jnp.einsum('blgc,gpc->blgp', uf, bbar_im)
    a_l_re = jnp.broadcast_to(abar_re, bu_re.shape)
    a_l_im = jnp.broadcast_to(abar_im, bu_im.shape)
    p_re, p_im, s_re, s_im = lax.associative_scan(
        _complex_affine_combine, (a_l_re, a_l_im, bu_re, bu_im), axis=1)
    h0r = h0_re.astype(f32)[:, None]
    h0i = h0_im.astype(f32)[:, None]
    h_re = s_re + p_re * h0r - p_im * h0i
    h_im = s_im + p_re * h0i + p_im * h0r
    y = (jnp.einsum('blgp,gcp->blgc', h_re, c_re.astype(f32))
         - jnp.einsum('blgp,gcp->blgc', h_im, c_im.astype(f32)))
    y = y.reshape(bsz, L, D_S5) + d_skip.astype(f32) * uf.reshape(bsz, L, D_S5)
    return y, h_re[:, -1], h_im[:, -1]

def mlstm_chunk(carry, blk):
    C, n, m = carry
    q, k, v, ig, lf = blk
    L = q.shape[2]
    b = jnp.cumsum(lf, axis=-1)
    causal = jnp.tril(jnp.ones((L, L), dtype=bool))
    dmat = jnp.where(causal, b[..., :, None] - b[..., None, :] + ig[..., None, :], -jnp.inf)
    inter = b + m[..., None]
    m_t = jnp.maximum(inter, jnp.max(dmat, axis=-1))
    w_inter = jnp.exp(inter - m_t)
    s = jnp.einsum('bhtd,bhsd->bhts', q, k) * jnp.exp(dmat - m_t[..., None])
    num = jnp.einsum('bhts,bhsd->bhtd', s, v) + w_inter[..., None] * jnp.einsum('bhvk,bhtk->bhtv', C, q)
    den_dot = jnp.sum(s, axis=-1) + w_inter * jnp.einsum('bhk,bhtk->bht', n, q)
    den = jnp.maximum(jnp.abs(den_dot), jnp.exp(-m_t))
    h = num / den[..., None]
    m_new = m_t[..., -1]
    w_end = jnp.exp(b[..., -1:] - b + ig - m_new[..., None])
    decay = jnp.exp(inter[..., -1] - m_new)
    C_new = decay[..., None, None] * C + jnp.einsum('bhs,bhsv,bhsk->bhvk', w_end, v, k)
    n_new = decay[..., None] * n + jnp.einsum('bhs,bhsk->bhk', w_end, k)
    return (C_new, n_new, m_new), h

def mixer(xn, h0_re, h0_im, C0, n0, m0, w_in, b_ig, b_fg, a_re, a_im, log_dt, b_re, b_im,
          c_re, c_im, d_skip, w_s5_glu, ml_gn, w_ml_out, w_out):
    f32 = jnp.float32
    bsz, L, _ = xn.shape
    splits = np.cumsum([D_S5, D_ML, D_ML, D_ML, D_ML, ML_HEADS, ML_HEADS, D_MODEL]).tolist()
    u, q, k, v, o, ig, fg, g_s5, g_ml = jnp.split(jnp.dot(xn, w_in), splits, axis=-1)
    y, hr, hi = s5_scan(u, h0_re, h0_im, a_re, a_im, log_dt, b_re, b_im, c_re, c_im, d_skip)
    glu = jnp.dot(jax.nn.gelu(y), w_s5_glu.astype(f32))
    y_s5 = glu[..., :D_MODEL] * jax.nn.sigmoid(glu[..., D_MODEL:])
    cl = min(CHUNK, L)
    nc = L // cl

    def to_chunks(t):
        return t.astype(f32).reshape(bsz, nc, cl, ML_HEADS, -1).transpose(1, 0, 3, 2, 4)

    qc = to_chunks(q) * (ML_HEAD_DIM ** -0.5)
    kc = to_chunks(k)
    vc = to_chunks(v)
    igc = to_chunks(ig.astype(f32) + b_ig.astype(f32))[..., 0]
    lfc = to_chunks(jax.nn.log_sigmoid(fg.astype(f32) + b_fg.astype(f32)))[..., 0]
    init = (C0.astype(f32), n0.astype(f32), m0.astype(f32))
    (C, n, m), hc = lax.scan(mlstm_chunk, init, (qc, kc, vc, igc, lfc))
    h = hc.transpose(1, 0, 3, 2, 4).reshape(bsz, L, ML_HEADS, ML_HEAD_DIM)
    hcent = h - jnp.mean(h, axis=-1, keepdims=True)
    hn = hcent * lax.rsqrt(jnp.mean(hcent * hcent, axis=-1, keepdims=True) + EPS)
    hn = hn.reshape(bsz, L, D_ML) * ml_gn.astype(f32)
    y_ml = jnp.dot(jax.nn.sigmoid(o.astype(f32)) * hn, w_ml_out.astype(f32))
    mix = jax.nn.sigmoid(g_s5.astype(f32)) * y_s5 + jax.nn.sigmoid(g_ml.astype(f32)) * y_ml
    out = jnp.dot(mix.astype(xn.dtype), w_out)
    return out, (hr, hi, C, n, m)

def moe(x, w_router, b_router, w_gate_up, b_gate_up, w_down, b_down):
    f32 = jnp.float32
    T = x.shape[0]
    logits = jnp.dot(x, w_router).astype(f32) + b_router.astype(f32)
    top_val, top_idx = lax.top_k(logits, TOP_K)
    gates = jax.nn.softmax(top_val, axis=-1)
    M = T * TOP_K
    flat_e = top_idx.reshape(M)
    order = jnp.argsort(flat_e)
    sorted_e = flat_e[order]
    counts = jnp.bincount(flat_e, length=N_EXPERTS)
    padded = (counts + MOE_BLOCK - 1) // MOE_BLOCK * MOE_BLOCK
    starts = jnp.cumsum(counts) - counts
    pends = jnp.cumsum(padded)
    pstarts = pends - padded
    dest_sorted = pstarts[sorted_e] + jnp.arange(M, dtype=jnp.int32) - starts[sorted_e]
    dest = jnp.zeros((M,), jnp.int32).at[order].set(dest_sorted.astype(jnp.int32))
    n_blocks = -(-(M + N_EXPERTS * (MOE_BLOCK - 1)) // MOE_BLOCK)
    buf = jnp.zeros((n_blocks * MOE_BLOCK, x.shape[1]), x.dtype).at[dest].set(jnp.repeat(x, TOP_K, axis=0))
    block_e = jnp.minimum(
        jnp.searchsorted(pends, jnp.arange(n_blocks, dtype=jnp.int32) * MOE_BLOCK, side='right'),
        N_EXPERTS - 1)

    def expert_block(args):
        xb, e = args
        gu = jnp.dot(xb, w_gate_up[e]) + b_gate_up[e]
        g = jnp.minimum(gu[:, :D_FF], SWIGLU_LIMIT)
        up = jnp.clip(gu[:, D_FF:], -SWIGLU_LIMIT, SWIGLU_LIMIT)
        hdn = (up + 1.0) * (g * jax.nn.sigmoid(SWIGLU_ALPHA * g))
        return jnp.dot(hdn, w_down[e]) + b_down[e]

    out_blocks = lax.map(expert_block, (buf.reshape(n_blocks, MOE_BLOCK, -1), block_e))
    out_rows = out_blocks.reshape(n_blocks * MOE_BLOCK, -1)
    y = jnp.einsum('tkd,tk->td', out_rows[dest].reshape(T, TOP_K, -1).astype(f32), gates)
    return y.astype(x.dtype)

def encoder_step(x, states, params):
    s5_re, s5_im, ml_C, ml_n, ml_m = states
    (norm_mix, w_in, b_ig, b_fg, s5_a_re, s5_a_im, s5_log_dt, s5_b_re, s5_b_im, s5_c_re, s5_c_im,
     s5_d, w_s5_glu, ml_gn, w_ml_out, w_out, norm_moe, w_router, b_router, w_gate_up, b_gate_up,
     w_down, b_down, norm_final) = params
    new_re, new_im, new_C, new_n, new_m = [], [], [], [], []
    for l in range(DEPTH):
        mix, (hr, hi, C, n, m) = mixer(
            rmsnorm(x, norm_mix[l]), s5_re[l], s5_im[l], ml_C[l], ml_n[l], ml_m[l],
            w_in[l], b_ig[l], b_fg[l], s5_a_re[l], s5_a_im[l], s5_log_dt[l], s5_b_re[l], s5_b_im[l],
            s5_c_re[l], s5_c_im[l], s5_d[l], w_s5_glu[l], ml_gn[l], w_ml_out[l], w_out[l])
        x = x + mix
        bsz, L, _ = x.shape
        ff = moe(rmsnorm(x, norm_moe[l]).reshape(bsz * L, D_MODEL), w_router[l], b_router[l],
                 w_gate_up[l], b_gate_up[l], w_down[l], b_down[l])
        x = x + ff.reshape(bsz, L, D_MODEL)
        new_re.append(hr)
        new_im.append(hi)
        new_C.append(C)
        new_n.append(n)
        new_m.append(m)
    y = rmsnorm(x, norm_final)
    return y, (jnp.stack(new_re), jnp.stack(new_im), jnp.stack(new_C), jnp.stack(new_n), jnp.stack(new_m))

def setup_inputs(seed: int = 0) -> dict:
    key = jax.random.key(seed)
    ks = jax.random.split(key, 32)
    f32 = jnp.float32

    def nrm(k, shape, scale):
        return jax.random.normal(k, shape, f32) * scale

    n_idx = jnp.arange(S5_STATE, dtype=f32)
    s5_shape = (DEPTH, S5_GROUPS, S5_STATE)
    return {
        'x_prompt': nrm(ks[0], (BATCH, SEQ, D_MODEL), 1.0),
        'x_sample': nrm(ks[1], (DEC_BATCH, DEC_SEQ, D_MODEL), 1.0),
        'state_s5_re': nrm(ks[2], (DEPTH, DEC_BATCH, S5_GROUPS, S5_STATE), 0.1),
        'state_s5_im': nrm(ks[3], (DEPTH, DEC_BATCH, S5_GROUPS, S5_STATE), 0.1),
        'state_ml_C': nrm(ks[4], (DEPTH, DEC_BATCH, ML_HEADS, ML_HEAD_DIM, ML_HEAD_DIM), 0.1),
        'state_ml_n': nrm(ks[5], (DEPTH, DEC_BATCH, ML_HEADS, ML_HEAD_DIM), 0.1),
        'state_ml_m': jax.random.uniform(ks[6], (DEPTH, DEC_BATCH, ML_HEADS), f32, 0.0, 4.0),
        'norm_mix': 1.0 + nrm(ks[7], (DEPTH, D_MODEL), 0.01),
        'w_in': nrm(ks[8], (DEPTH, D_MODEL, D_IN), D_MODEL ** -0.5),
        'b_ig': nrm(ks[9], (DEPTH, ML_HEADS), 0.1) - 1.0,
        'b_fg': jnp.linspace(3.0, 6.0, ML_HEADS, dtype=f32) + nrm(ks[10], (DEPTH, ML_HEADS), 0.1),
        's5_a_re': -0.5 + nrm(ks[11], s5_shape, 0.01),
        's5_a_im': math.pi * n_idx + nrm(ks[12], s5_shape, 0.01),
        's5_log_dt': jax.random.uniform(ks[13], (DEPTH, S5_GROUPS), f32, math.log(1e-3), math.log(1e-1)),
        's5_b_re': nrm(ks[14], (DEPTH, S5_GROUPS, S5_STATE, S5_GROUP), (2 * S5_GROUP) ** -0.5),
        's5_b_im': nrm(ks[15], (DEPTH, S5_GROUPS, S5_STATE, S5_GROUP), (2 * S5_GROUP) ** -0.5),
        's5_c_re': nrm(ks[16], (DEPTH, S5_GROUPS, S5_GROUP, S5_STATE), (2 * S5_STATE) ** -0.5),
        's5_c_im': nrm(ks[17], (DEPTH, S5_GROUPS, S5_GROUP, S5_STATE), (2 * S5_STATE) ** -0.5),
        's5_d': nrm(ks[18], (DEPTH, D_S5), 1.0),
        'w_s5_glu': nrm(ks[19], (DEPTH, D_S5, 2 * D_MODEL), D_S5 ** -0.5),
        'ml_gn': 1.0 + nrm(ks[20], (DEPTH, D_ML), 0.01),
        'w_ml_out': nrm(ks[21], (DEPTH, D_ML, D_MODEL), D_ML ** -0.5),
        'w_out': nrm(ks[22], (DEPTH, D_MODEL, D_MODEL), D_MODEL ** -0.5),
        'norm_moe': 1.0 + nrm(ks[23], (DEPTH, D_MODEL), 0.01),
        'w_router': nrm(ks[24], (DEPTH, D_MODEL, N_EXPERTS), D_MODEL ** -0.5),
        'b_router': nrm(ks[25], (DEPTH, N_EXPERTS), 0.01),
        'w_gate_up': nrm(ks[26], (DEPTH, N_EXPERTS, D_MODEL, 2 * D_FF), D_MODEL ** -0.5),
        'b_gate_up': nrm(ks[27], (DEPTH, N_EXPERTS, 2 * D_FF), 0.01),
        'w_down': nrm(ks[28], (DEPTH, N_EXPERTS, D_FF, D_MODEL), D_FF ** -0.5),
        'b_down': nrm(ks[29], (DEPTH, N_EXPERTS, D_MODEL), 0.01),
        'norm_final': 1.0 + nrm(ks[30], (D_MODEL,), 0.01),
    }

def reference(x_prompt, x_sample, state_s5_re, state_s5_im, state_ml_C, state_ml_n, state_ml_m,
              norm_mix, w_in, b_ig, b_fg, s5_a_re, s5_a_im, s5_log_dt, s5_b_re, s5_b_im,
              s5_c_re, s5_c_im, s5_d, w_s5_glu, ml_gn, w_ml_out, w_out, norm_moe, w_router,
              b_router, w_gate_up, b_gate_up, w_down, b_down, norm_final):
    params = (norm_mix, w_in, b_ig, b_fg, s5_a_re, s5_a_im, s5_log_dt, s5_b_re, s5_b_im, s5_c_re,
              s5_c_im, s5_d, w_s5_glu, ml_gn, w_ml_out, w_out, norm_moe, w_router, b_router,
              w_gate_up, b_gate_up, w_down, b_down, norm_final)
    bp = x_prompt.shape[0]
    f32 = jnp.float32
    zero_states = (jnp.zeros((DEPTH, bp, S5_GROUPS, S5_STATE), f32),
                   jnp.zeros((DEPTH, bp, S5_GROUPS, S5_STATE), f32),
                   jnp.zeros((DEPTH, bp, ML_HEADS, ML_HEAD_DIM, ML_HEAD_DIM), f32),
                   jnp.zeros((DEPTH, bp, ML_HEADS, ML_HEAD_DIM), f32),
                   jnp.zeros((DEPTH, bp, ML_HEADS), f32))
    y_prompt, (p_re, p_im, p_C, p_n, p_m) = encoder_step(x_prompt, zero_states, params)
    y_sample, (s_re, s_im, s_C, s_n, s_m) = encoder_step(
        x_sample, (state_s5_re, state_s5_im, state_ml_C, state_ml_n, state_ml_m), params)
    return (y_prompt, y_sample, p_re, p_im, p_C, p_n, p_m, s_re, s_im, s_C, s_n, s_m)


_drawn_inputs = setup_inputs


def setup_inputs(seed=0):
    import zlib

    import numpy as np

    out = dict(_drawn_inputs(seed))
    spreads = {}
    factors = {'s5_a_re': 4.318, 'b_gate_up': 8.0, 'b_down': 8.0, 'norm_final': 5.538}
    for name, (base, spread) in spreads.items():
        noise = np.random.default_rng([zlib.crc32(name.encode()), seed]).standard_normal(out[name].shape)
        drawn = base * np.exp(spread * noise) if base else spread * noise
        out[name] = __import__('jax').numpy.asarray(drawn.astype(out[name].dtype))
    for name, factor in factors.items():
        out[name] = (out[name] * factor).astype(out[name].dtype)
    return out
```

```python
from contextlib import ExitStack

import numpy as np

import concourse.bass as bass
from concourse import mybir

P = 128
ALU = mybir.AluOpType
ACT = mybir.ActivationFunctionType
AX_X = mybir.AxisListType.X
F32 = mybir.dt.float32
BF16 = mybir.dt.bfloat16
I32 = mybir.dt.int32
U32 = mybir.dt.uint32

D = 1024
DK = D // P
TP, TS = 256, 64
T = TP + TS
TILES = [(0, 128), (128, 128), (256, 64)]
CH = 64
NC = T // CH
NCP = TP // CH
DS5, S5G, S5C, S5P = 512, 32, 16, 64
NJ = S5G * S5P // P
H, HD = 4, 128
NE, TOPK, FF = 32, 4, 1024
FK = FF // P
SLOT = 64
MAXB = -(-T // SLOT)
EPS = 1e-6
LIMIT, ALPHA = 7.0, 1.702
D_IN = DS5 + 4 * H * HD + 2 * H + 2 * D
GATE0 = DS5 + 4 * H * HD
TWO_PI = 6.283185307179586
PI2_A = 6.28125
PI2_B = float(np.float32(np.round((TWO_PI - PI2_A) * 2 ** 21) / 2 ** 21))
PI2_C = TWO_PI - PI2_A - PI2_B
PI_IN = 3.1415925
ROUND = 1.5 * 2 ** 23

C_ID, C_TRI, C_ONE, C_SLOT, C_EXP = 0, 128, 256, 384, 512
C_KEEP = 544
C_CAUSAL, C_PAR, C_HEAD, C_SEG = 544, 608, 610, 1122
C_ALL = C_SEG + T

CHUNK = 2048
GU_CHUNKS, DN_CHUNKS = DK, FK // 2
CHUNKS = GU_CHUNKS + DN_CHUNKS


def shape_constants():
    c = np.zeros((P, C_ALL), np.float32)
    r = np.arange(P)
    c[:, C_ID:C_ID + P] = np.eye(P)
    c[:, C_TRI:C_TRI + P] = r[:, None] < r[None, :]
    c[:, C_ONE:C_ONE + P] = 1.0
    c[:, C_SLOT:C_SLOT + P] = (r % SLOT)[None, :]
    c[:, C_EXP:C_EXP + NE] = np.arange(NE)[None, :]
    s = np.arange(CH)
    c[:CH, C_CAUSAL:C_CAUSAL + CH] = np.where(s[:, None] <= s[None, :], 0.0, -1e30)
    for par in range(2):
        c[:, C_PAR + par] = (r // S5C) % 2 == par
    for h in range(H):
        c[h, C_HEAD + h * P:C_HEAD + (h + 1) * P] = 1.0
    c[:H, C_SEG:C_SEG + T] = (np.arange(T) % CH != 0)[None, :]
    return c


def hybrid_stream_step(nc, a, out):
    with ExitStack() as ctx:
        def sb(name, shape, dt=F32):
            return ctx.enter_context(nc.sbuf_tensor(name, shape, dt))

        sems = {}

        def S(name):
            if name not in sems:
                sems[name] = ctx.enter_context(nc.semaphore(name))
            return sems[name]

        class Order:

            def __init__(self, eng, name):
                self.eng, self.sem, self.count = eng, S(name), 0

            def start(self, ins):
                self.count += 1
                ins.then_inc(self.sem, 1)

            def wait(self):
                self.eng.wait_ge(self.sem, self.count)

            def __call__(self, ins):
                self.start(ins)
                self.wait()

        ring = sb("ring", [P, CHUNKS * CHUNK])
        m2 = sb("m2", [P, 12288])
        acc = sb("acc", [P, 3, D])
        xnT = sb("xnT", [P, DK, T])
        uT = sb("uT", [P, 4, T])
        oT = sb("oT", [P, 4, T])
        gates = sb("gates", [P, 2, DK, T])
        bg = sb("bg", [P, NE, 2, FK])
        cst = sb("cst", [P, C_KEEP])
        vc = sb("vc", [P, 16])
        st = sb("st", [P, 24])
        tab = sb("tab", [P, NE, 6])
        sm = sb("sm", [P, 640])
        rm = sb("rm", [H, T])
        cum = sb("cum", [1, NE + 1], I32)
        cumf = sb("cumf", [1, 4, NE + 1])
        psum = ctx.enter_context(nc.psum_tensor("psum", [P, 8, 512], F32))
        PJ = [psum[:, 0], psum[:, 1]]
        GU, DN, XB, PTB, CB = 0, 2, 4, 5, 6

        ident = cst[:, C_ID:C_ID + P]
        ones = cst[:, C_ONE:C_ONE + P]

        def flat(t):
            n = len(t.shape)
            if n == 2:
                return t[:, :]
            names = " ".join("abcde"[:n - 1])
            return t.rearrange(f"p {names} -> p ({names})")

        def cut(ap, *dims):
            names = "abcde"[:len(dims)]
            return ap.rearrange(f"p ({' '.join(names)}) -> p {' '.join(names)}", **dict(zip(names, dims)))

        class Space:
            def __init__(self, buf, start=0, end=None):
                self.buf, self.at, self.end = buf, start, end or buf.shape[1]

            def take(self, *dims):
                n = int(np.prod(dims))
                self.at += n
                assert self.at <= self.end
                return cut(self.buf[:, self.at - n:self.at], *dims) if len(dims) > 1 else self.buf[:, self.at - n:self.at]

        r = Space(ring)
        ct = r.take(NJ, T)
        sn = r.take(NJ, T)
        btz = r.take(2, NJ, P)
        ctt = r.take(2, 4, P)
        WORK = r.at
        zz = r.take(2, 2, T)
        dtmp = r.take(2, T)
        ptmp = r.take(2, T)
        hh = r.take(2, 2, T)
        WORK_END = r.at
        qT, kT, vT = r.take(4, T), r.take(4, T), r.take(4, T)
        wg = r.take(DK, 36)
        cst2 = r.take(C_ALL - C_KEEP)
        w = Space(ring, WORK, WORK_END)
        bnat, bpad = w.take(2, NJ, S5C), w.take(2, NJ, 32)
        cnat, cpad = w.take(2, 4, S5P), w.take(2, 4, 2, S5P)
        w = Space(ring, WORK, WORK_END)
        num = w.take(H, HD + 1)[0:CH]
        hn = w.take(H, HD)[0:CH]
        vw = w.take(H, HD + 1)[0:CH]
        w = Space(ring)
        stage = [(w.take(H, HD), w.take(HD)[0:H]) for _ in range(2)]
        stage5 = w.take(4, P)[0:NJ]
        w = Space(flat(gates[:, :, :, :]))
        prm = w.take(20, P)[0:NJ]
        (A_RE, A_IM, H0R, H0I, DAI, RED, MAG, COS, SIN, FR, FI, X0, X1, X2, DEN, LDT) = range(16)
        btmp = w.take(4, P)
        vecs = w.take(P)[0:16]
        c0n = w.take(H, P)
        n0n = w.take(P)[0:H]
        gS, gM = gates[:, 0], gates[:, 1]

        wr = cut(m2[:, 0:3 * CHUNK], 3, CHUNK)
        w = Space(m2, 3 * CHUNK)
        xn = w.take(3, D)
        w = Space(m2, 3 * CHUNK)
        ttmp = [w.take(NJ // 2, P), w.take(NJ // 2, P)]
        btmp2 = w.take(4, NJ, S5C)
        w = Space(m2, 3 * CHUNK)
        kn = w.take(NC, H, HD)[0:CH]
        wt = w.take(H, NC, CH)[0:CH]
        cn = w.take(2, H, HD + 1)
        cn0 = w.take(H, HD + 1)
        gtmp = m2[:, m2.shape[1] - T:]
        vn = cut(flat(acc[:, :, :])[0:CH, 0:NC * H * (HD + 1)], NC, H, HD + 1)

        w = Space(m2, 0, 3 * CHUNK)
        gus = w.take(2 * 512)
        hb = w.take(FK, 2, SLOT)
        osb = w.take(2 * 512)
        xeT, sg, hT = w.take(DK, SLOT), w.take(FK, SLOT), w.take(FK, SLOT)
        pb = cut(w.take(96).bitcast(BF16), 3, SLOT)
        pw = w.take(3, P)
        pt = w.take(T)
        cur = w.take(6)
        w = Space(m2, 3 * CHUNK)
        parts = cut(w.take(3 * 3 * D // 2).bitcast(BF16), 3, 3, D)
        nmb = w.take(D)
        square1 = cut(m2[:, CHUNK:CHUNK + 3 * D], 3, D)
        square2 = cut(m2[:, 0:3 * D], 3, D)
        nfb = flat(uT[:, :, :])[:, 0:D]
        w = Space(flat(gates[:, :, :, :]))
        xm = w.take(3, D)
        bdn, gT = w.take(D)[0:NE], w.take(T)[0:NE]
        wrt = w.take(DK, NE)
        brt = w.take(NE)

        w = Space(sm)
        pcol = w.take(7, NJ)
        M_FR, M_FI, M_MAG, M_COS, M_SIN, M_H0R, M_H0I = range(7)
        fin = w.take(4, NJ)
        wcol = w.take(3, NC, H)[0:CH]
        dec = w.take(H, NC)
        bns, mv = w.take(H, 6), w.take(H, 2)
        den = w.take(2 * H)
        bcol = w.take(2)
        top = [(w.take(NE), w.take(8), w.take(8).bitcast(U32), w.take(16)) for _ in TILES]
        msk = w.take(3, NE)
        tk = w.take(NE)
        (R_IG, R_LF, R_B, R_M, R_A, R_AL, R_WI, R_WE) = range(8)

        rows = [oT[0:H, k, :] for k in range(4)]
        rows += [flat(cn)[0:H, k * T:(k + 1) * T] for k in range(3)]
        rows.insert(R_M, rm[:, :])

        def by_chunk(k):
            return cut(rows[k], NC, CH)

        x_rows = [a["x_prompt"][0, 0:128, :], a["x_prompt"][0, 128:256, :], a["x_sample"][0, :, :]]
        y_rows = [out[0][0, 0:128, :], out[0][0, 128:256, :], out[1][0, :, :]]
        w_in = a["w_in"][0].rearrange("(k p) n -> p k n", p=P)
        w_glu = a["w_s5_glu"][0].rearrange("(k p) n -> p k n", p=P)
        w_ml = a["w_ml_out"][0].rearrange("(k p) n -> p k n", p=P)
        w_out = a["w_out"][0].rearrange("(k p) n -> p k n", p=P)

        groups = []
        for g in range(18):
            c = 256 * g if g < 10 else GATE0 + 2 * H + 256 * (g - 10)
            groups.append([(DK, 0, w_in[:, :, c:c + 256])])
        for g in range(4):
            groups.append([(4, 0, w_glu[:, :, 256 * g:256 * g + 256]),
                           (4, 256, w_glu[:, :, D + 256 * g:D + 256 * g + 256])])
        for g in range(2):
            groups.append([(4, 0, w_ml[:, :, 512 * g:512 * g + 512])])
        for g in range(4):
            groups.append([(DK, 0, w_out[:, :, 256 * g:256 * g + 256])])
        landed, total = [], [0, 0, 0]
        for g, dmas in enumerate(groups):
            total[g % 3] += 16 * len(dmas)
            landed.append(total[g % 3])
        G_IN, G_GLU, G_ML, G_OUT = 0, 18, 22, 24
        T_GLU, T_ML, T_OUT = 36, 52, 60

        S5_AT, ML_AT = 9, 28
        plan = {j: [] for j in range(T_ML)}
        for j, step in ((2, "s5_columns"), (3, "gate_rows"), (4, "biases"), (4, "state_in"), (5, "c_matrix"),
                        (6, "b_matrix"), (7, "row_columns")):
            plan[j].append((step, 0))
        plan[8] += [("decay_matrix", h) for h in range(H)]
        for j in range(NJ + 2):
            if j < NJ:
                plan[S5_AT + j].append(("s5_in", j))
            if j >= 2:
                plan[S5_AT + j].append(("s5_out", j - 2))
        for c in range(NC):
            plan[17 + c].append(("natural", c))
        for h in range(H):
            plan[22 + h].append(("scores", h))
        for c in range(NCP):
            plan[ML_AT + 2 * c].append(("chunk", c))
            plan[ML_AT + 2 * c + 2].append(("turn", c))
        plan[36] += [("states_out", 0)]
        plan[37] += [("chunk", NCP)]
        plan[39] += [("turn", NCP)]
        plan[40] += [("states_out", 1), ("s5_out_states", 0)]
        for j in plan:
            plan[j].sort(key=lambda s: s[0] == "chunk")

        block = ctx.enter_context(nc.Block())

        def expert_chunk(eng, c, e):
            dst = ring[:, c * CHUNK:(c + 1) * CHUNK]
            if c < GU_CHUNKS:
                src = a["w_gate_up"][0, bass.ds(e, 1), c * P:(c + 1) * P, :].rearrange("a p n -> p (a n)")
            else:
                k = 2 * (c - GU_CHUNKS)
                src = a["w_down"][0, bass.ds(e, 1), k * P:(k + 2) * P, :].rearrange("a (k p) n -> p (a k) n", p=P)
                dst = cut(dst, 2, D)
            eng.dma_start(dst, src).then_inc(S(f"w_landed{c}"), 16)

        @block.sync
        def _(sp):
            for i, (t0, n) in enumerate(TILES):
                sp.dma_start(acc[0:n, i, :], x_rows[i]).then_inc(S(f"x_landed{i}"), 16)
            sp.dma_start(cst[:, :], a["consts"][:, 0:C_KEEP]).then_inc(S("cst_landed"), 16)
            for g, dmas in enumerate(groups):
                if g >= 3:
                    sp.wait_ge(S("group_used"), g - 2)
                for kk, c0, src in dmas:
                    dst = cut(wr[:, g % 3], kk, CHUNK // kk)[:, :, c0:c0 + src.shape[2]]
                    sp.dma_start(dst, src).then_inc(S(f"slot_landed{g % 3}"), 16)
                if g == 23:
                    sp.wait_ge(S("hT_read"), NC)
                    sp.wait_ge(S("cn_ready"), NC)
                    sp.wait_ge(S("co_read"), 4)
                    for i, (t0, n) in enumerate(TILES):
                        sp.dma_start(acc[0:n, i, :], x_rows[i]).then_inc(S("res_landed"), 16)
                    sp.dma_start(nmb, a["norm_moe"][0:1, :].to_broadcast([P, D])).then_inc(S("nmb_landed"), 16)
                if g >= 24:
                    sp.wait_ge(S("states_stored"), 160)
                    for c in range((g - 24) * 3, (g - 23) * 3):
                        expert_chunk(sp, c, 0)
                if g == 26:
                    sp.wait_ge(S("mix_ready"), 8)
                    sp.dma_start(wrt, a["w_router"][0].rearrange("(k p) e -> p k e", p=P)).then_inc(S("wrt_landed"), 16)
                    sp.dma_start(brt, a["b_router"][0:1, :].to_broadcast([P, NE])).then_inc(S("wrt_landed"), 16)
                    sp.dma_start(bdn, a["b_down"][0]).then_inc(S("bdn_landed"), 16)
            sp.wait_ge(S("pj_done"), 72)
            sp.dma_start(nfb, a["norm_final"].rearrange("(a d) -> a d", a=1).to_broadcast([P, D])).then_inc(S("nfb_landed"), 16)
            sp.wait_ge(S("cum_ready"), 1)
            with sp.Fori(1, NE) as e:
                before = sp.value_load(cum[0:1, bass.ds(e, 1)], min_val=1, max_val=NE * MAXB)
                for c in range(CHUNKS):
                    sp.wait_ge(S("chunks_used"), before * CHUNKS + (c + 1))
                    expert_chunk(sp, c, e)
            for i, (t0, n) in enumerate(TILES):
                sp.wait_ge(S("y_ready"), i + 1)
                sp.dma_start(y_rows[i], acc[0:n, i, :]).then_inc(S("y_stored"), 16)
            sp.wait_ge(S("y_stored"), 48)

        @block.tensor
        def _(pe):
            def turn(dst, src, n):
                return pe.transpose(dst, src, ident[0:n, 0:n])

            def head(h, n):
                c = C_HEAD - C_KEEP + h * P
                return cst2[0:H, c:c + n]

            def project(j, g, kk, rhs, col):
                pe.wait_ge(S(f"slot_landed{g % 3}"), landed[g])
                if j >= 2:
                    pe.wait_ge(S(f"pj_free{j % 2}"), j // 2)
                w = cut(wr[:, g % 3], kk, CHUNK // kk)
                for k in range(kk):
                    mm = pe.matmul(PJ[j % 2][:, 0:T], w[:, k, col:col + P], rhs[:, k, :], start=(k == 0), stop=(k == kk - 1))
                mm.then_inc(S("pj_done"), 1)

            def group_used(j):
                pe.wait_ge(S("pj_done"), j + 1)
                pe.sem_inc(S("group_used"), 1)

            def s5_columns(_):
                pe.wait_ge(S("prm_ready"), 1)
                for n, k in enumerate((FR, FI, MAG, COS, SIN, H0R, H0I)):
                    mm = turn(psum[:, 2, n * NJ:(n + 1) * NJ], prm[:, k, :], NJ)
                mm.then_inc(S("prmT"), 1)

            def gate_rows(_):
                pe.wait_ge(S("wg_landed"), 32)
                for k in range(DK):
                    mm = pe.matmul(psum[0:36, 5, 0:T], wg[:, k, :], xnT[:, k, :], start=(k == 0), stop=(k == DK - 1))
                mm.then_inc(S("gate_mm"), 1)

            def biases(_):
                pe.wait_ge(S("btmp_landed"), 16)
                for q in range(4):
                    mm = turn(psum[:, 3, q * P:(q + 1) * P], btmp[:, q, :], P)
                mm.then_inc(S("bgT"), 1)

            def state_in(_):
                pe.wait_ge(S("c0_landed"), 32)
                for h in range(H):
                    turn(psum[:, 6, h * P:(h + 1) * P], c0n[:, h, :], P)
                turn(psum[:, 7, 0:H], n0n, H).then_inc(S("c0T"), 1)

            def c_matrix(_):
                pe.wait_ge(S("cpad_ready"), 1)
                pe.wait_ge(S("cn0_ready"), 1)
                for k in range(2):
                    for q in range(4):
                        mm = turn(psum[:, 6 + k, q * P:(q + 1) * P], flat(cpad[:, k, q]), P)
                mm.then_inc(S("cT"), 1)

            def b_matrix(_):
                pe.wait_ge(S("bpad_ready"), 1)
                pe.wait_ge(S("ctt_ready"), 1)
                for k in range(2):
                    for q in range(4):
                        mm = turn(psum[:, 6 + k, q * P:(q + 1) * P], flat(bpad[:, k, 4 * q:4 * q + 4]), P)
                mm.then_inc(S("bT"), 1)

            def row_columns(_):
                pe.wait_ge(S("rows_ready"), 1)
                pe.wait_ge(S("pcol_ready"), 1)
                pe.wait_ge(S("bg_ready"), 1)
                for n, k in enumerate((R_WI, R_WE, R_M)):
                    for c in range(NC):
                        o = (n * NC + c) * H
                        turn(psum[0:CH, 2, o:o + H], by_chunk(k)[:, c, :], H)
                for h in range(H):
                    mm = pe.matmul(psum[:, 3, h * NC:(h + 1) * NC], head(h, P), by_chunk(R_WI)[:, :, CH - 1], start=True, stop=True)
                mm.then_inc(S("cols_mm"), 1)

            def decay_matrix(h):
                if h == 0:
                    pe.wait_ge(S("btz_ready"), 1)
                if h >= 2:
                    pe.wait_ge(S("dm_read"), h - 1)
                b = 6 + h % 2
                pe.matmul(psum[0:CH, b, 0:T], head(h, CH), rows[R_AL], start=True, stop=False, skip_group_check=True)
                for c in range(NC):
                    mm = pe.matmul(psum[0:CH, b, c * CH:(c + 1) * CH], by_chunk(R_A)[:, c, :], head(h, CH),
                                   start=False, stop=(c == NC - 1), skip_group_check=True)
                mm.then_inc(S("dm_done"), 1)

            def s5_in(j):
                if j == 0:
                    pe.wait_ge(S("cols_ready"), 1)
                    pe.wait_ge(S("u_ready"), 1)
                else:
                    pe.wait_ge(S("bu_read"), j)
                for k in range(2):
                    mm = pe.matmul(psum[:, 2 + k, 0:T], btz[:, k, j, :], uT[:, j // 4, :], start=True, stop=True)
                mm.then_inc(S("bu_done"), 1)

            def s5_out(j):
                q, t = j % 4, j // 4
                pe.wait_ge(S("h_ready"), j + 1)
                if q == 0 and t > 0:
                    pe.wait_ge(S("y_read"), t)
                for k in range(2):
                    mm = pe.matmul(psum[32 * q:32 * q + 32, 4, 0:T], ctt[:, k, t, 32 * q:32 * q + 32], hh[:, j % 2, k, :],
                                   start=(k == 0), stop=(k == 1))
                mm.then_inc(S("y_done"), 1)

            def natural(c):
                for n, src in enumerate((kT, vT)):
                    i = 2 * c + n
                    if i == 0:
                        pe.wait_ge(S("qkv_ready"), 1)
                        pe.wait_ge(S("dm_read"), 4)
                    if i >= 2:
                        pe.wait_ge(S("nat_read"), i - 1)
                    for h in range(H):
                        mm = turn(psum[0:CH, 6 + i % 2, h * P:(h + 1) * P], src[:, h, c * CH:(c + 1) * CH], P)
                    mm.then_inc(S("nat_done"), 1)

            def scores(h):
                if h == 0:
                    pe.wait_ge(S("nat_read"), 2 * NC)
                if h >= 2:
                    pe.wait_ge(S("st_ready"), h - 1)
                for c in range(NC):
                    mm = pe.matmul(psum[0:CH, 6 + h % 2, c * CH:(c + 1) * CH], kT[:, h, c * CH:(c + 1) * CH],
                                   qT[:, h, c * CH:(c + 1) * CH], start=True, stop=True)
                mm.then_inc(S("sc_done"), 1)

            def two(b, h, n):
                return psum[0:n, b + h // 2, (h % 2) * (HD + 1):(h % 2 + 1) * (HD + 1)]

            def chunk(c):
                if c == 0:
                    pe.wait_ge(S("st_ready"), H)
                    pe.wait_ge(S("y_read"), 4)
                    pe.wait_ge(S("bu_read"), NJ)
                else:
                    pe.wait_ge(S("hT_read"), c)
                for h in range(H):
                    mm = pe.matmul(two(2, h, CH), wt[:, h, c, :], vn[:, c, h, :], start=True, stop=True)
                mm.then_inc(S("a_done"), 1)
                if c > 0:
                    if c < NCP:
                        pe.wait_ge(S("cn_ready"), c)
                    state = cn[:, c % 2] if c < NCP else cn0
                    for h in range(H):
                        mm = pe.matmul(two(4, h, CH), qT[:, h, c * CH:(c + 1) * CH], state[:, h, :], start=True, stop=True)
                    mm.then_inc(S("b_done"), 1)
                pe.wait_ge(S("vw_ready"), c + 1)
                if c == NCP:
                    pe.wait_ge(S("co_read"), 2)
                for h in range(H):
                    mm = pe.matmul(two(6, h, P), kn[:, c, h, :], vw[:, h, :], start=True, stop=True)
                mm.then_inc(S("u_done"), 1)

            def turn_chunk(c):
                pe.wait_ge(S("hn_ready"), c + 1)
                for h in range(H):
                    mm = turn(psum[:, 2, h * CH:(h + 1) * CH], hn[:, h, :], CH)
                mm.then_inc(S("hT_done"), 1)

            def states_out(s):
                pe.wait_ge(S("cn_ready"), NCP + s)
                if s == 1:
                    pe.wait_ge(S("co_read"), 2)
                for h in range(H):
                    turn(psum[:, 6, h * P:(h + 1) * P], cn[:, s, h, 0:HD], P)
                turn(psum[0:H, 7, 0:P], cn[:, s, :, HD], P).then_inc(S("co_done"), 1)

            def s5_out_states(_):
                pe.wait_ge(S("fin_ready"), 2 * NJ)
                pe.wait_ge(S("hT_read"), NC)
                for n in range(4):
                    mm = turn(psum[0:NJ, 2, n * P:(n + 1) * P], fin[:, n, :], P)
                mm.then_inc(S("finT"), 1)

            steps = dict(s5_columns=s5_columns, gate_rows=gate_rows, biases=biases, state_in=state_in,
                         c_matrix=c_matrix, b_matrix=b_matrix, row_columns=row_columns, decay_matrix=decay_matrix,
                         s5_in=s5_in, s5_out=s5_out, natural=natural, scores=scores, chunk=chunk, turn=turn_chunk,
                         states_out=states_out, s5_out_states=s5_out_states)

            pe.wait_ge(S("cst_landed"), 16)
            pe.wait_ge(S("vecs_landed"), 48)
            turn(psum[:, 0, 0:16], vecs, 16).then_inc(S("vcT"), 1)
            for i, (t0, n) in enumerate(TILES):
                pe.wait_ge(S("xn_ready"), i + 1)
                for k in range(DK):
                    mm = turn(psum[:, 2 + 2 * i + k // 4, (k % 4) * P:(k % 4) * P + n], xn[0:n, i, k * P:(k + 1) * P], n)
                mm.then_inc(S("xT"), 1)
            pe.wait_ge(S("xnT_ready"), 3)
            pe.wait_ge(S("vc_ready"), 1)
            for j in range(T_GLU):
                project(j, j // 2, DK, xnT, (j % 2) * P)
                if j % 2 == 1:
                    group_used(j)
                if j == 2:
                    pe.wait_ge(S("cst2_landed"), 16)
                for step, i in plan[j]:
                    steps[step](i)
            pe.wait_ge(S("gelu_ready"), 4)
            for i in range(16):
                j = T_GLU + i
                project(j, G_GLU + i // 4, 4, uT, (i % 4 // 2) * P + (i % 2) * 256)
                if i % 4 == 3:
                    group_used(j)
                for step, n in plan[j]:
                    steps[step](n)
            pe.wait_ge(S("hT_read"), NC)
            for i in range(8):
                j = T_ML + i
                project(j, G_ML + i // 4, 4, oT, (i % 4) * P)
                if i % 4 == 3:
                    group_used(j)
            pe.wait_ge(S("mix_ready"), 8)
            j = T_OUT
            for g in range(G_OUT, G_OUT + 4):
                pe.wait_ge(S(f"slot_landed{g % 3}"), landed[g])
                for i, (t0, n) in enumerate(TILES):
                    pe.wait_ge(S(f"pj_free{j % 2}"), j // 2)
                    for k in range(DK):
                        mm = pe.matmul(PJ[j % 2][0:n, 0:256], gS[:, k, t0:t0 + n], cut(wr[:, g % 3], DK, 256)[:, k, :],
                                       start=(k == 0), stop=(k == DK - 1))
                    mm.then_inc(S("pj_done"), 1)
                    j += 1
                group_used(j - 1)

            for i, (t0, n) in enumerate(TILES):
                pe.wait_ge(S("xm_ready"), i + 1)
                for k in range(DK):
                    mm = turn(psum[:, 2 + 2 * i + k // 4, (k % 4) * P:(k % 4) * P + n], xm[0:n, i, k * P:(k + 1) * P], n)
                mm.then_inc(S("xmT"), 1)
            pe.wait_ge(S("wrt_landed"), 32)
            for i, (t0, n) in enumerate(TILES):
                pe.wait_ge(S("xmT_ready"), i + 1)
                for k in range(DK):
                    mm = pe.matmul(psum[0:n, i, 0:NE], xnT[:, k, t0:t0 + n], wrt[:, k, :],
                                   start=(k == 0), stop=(k == DK - 1))
                mm.then_inc(S("logits"), 1)
            pe.wait_ge(S("mask_ready"), 3)
            for i, (t0, n) in enumerate(TILES):
                for b in range(i + 1):
                    nb = TILES[b][1]
                    before = cst[0:nb, C_TRI:C_TRI + n] if b == i else ones[0:nb, 0:n]
                    pe.matmul(psum[0:n, 4, i * NE:(i + 1) * NE], before, msk[0:nb, b, :], start=(b == 0), stop=(b == i))
            for b in range(3):
                nb = TILES[b][1]
                mm = pe.matmul(psum[0:1, 3, 0:NE], ones[0:nb, 0:1], msk[0:nb, b, :], start=(b == 0), stop=(b == 2))
            mm.then_inc(S("ranks"), 1)
            pe.wait_ge(S("tab_ready"), 3)
            for i, (t0, n) in enumerate(TILES):
                mm = turn(psum[0:NE, 5, t0:t0 + n], tab[0:n, :, 3 + i], n)
            mm.then_inc(S("gTp"), 1)
            pe.wait_ge(S("gT_ready"), 1)
            pe.wait_ge(S("bdn_landed"), 16)
            for i, (t0, n) in enumerate(TILES):
                for hf in range(2):
                    if i > 0:
                        pe.wait_ge(S("bias_added"), 2 * i + hf - 1)
                    pe.matmul(psum[0:n, 6 + hf, :], gT[:, t0:t0 + n], bdn[:, hf * 512:(hf + 1) * 512],
                              start=True, stop=True).then_inc(S("bias_mm"), 1)

            def gather(g):
                pe.wait_ge(S("p_ready"), g + 1)
                for k in range(DK):
                    for i in range(3):
                        for q in range(3):
                            mm = pe.matmul(psum[:, XB, k * SLOT:(k + 1) * SLOT], parts[:, q, i, k * P:(k + 1) * P], pb[:, i, :],
                                           start=(i == 0 and q == 0), stop=(i == 2 and q == 2))
                mm.then_inc(S("gathered"), 1)

            def combine(g):
                pe.wait_ge(S("osb_ready"), 2 * g + 2)
                pe.wait_ge(S("pt_ready"), g + 1)
                for i, (t0, n) in enumerate(TILES):
                    for hf in range(2):
                        pe.wait_ge(S("added"), 6 * g + 2 * i + hf + 1)
                        pe.matmul(psum[0:n, CB + hf, :], pt[:, t0:t0 + n], osb[:, hf * 512:(hf + 1) * 512],
                                  start=True, stop=True).then_inc(S("combined"), 1)

            pe.wait_ge(S("parts_ready"), 3)
            gather(0)
            pe.wait_ge(S("cum_ready"), 1)
            with pe.Fori(0, NE) as e:
                first = pe.value_load(cum[0:1, bass.ds(e, 1)], min_val=0, max_val=NE * MAXB)
                end = pe.value_load(cum[0:1, bass.ds(e + 1, 1)], min_val=1, max_val=NE * MAXB)
                with pe.Fori(first, end) as g:
                    pe.wait_ge(S("xe_ready"), g + 1)
                    pe.wait_ge(S("gus_ready"), 2 * g + 2)
                    for c in range(GU_CHUNKS):
                        pe.wait_ge(S(f"w_landed{c}"), 16 * e + 16)
                        for hf in range(2):
                            for gu in range(2):
                                base = c * CHUNK + gu * FF + hf * 512
                                mm = pe.matmul(psum[64 * gu:64 * gu + 64, GU + hf, :], xeT[:, c, :], ring[:, base:base + 512],
                                               start=(c == 0), stop=(c == GU_CHUNKS - 1))
                        mm.then_inc(S("chunks_used"), 1)
                    gather(g + 1)
                    pe.wait_ge(S("gus_ready"), 2 * g + 4)
                    pe.wait_ge(S("osb_ready"), 2 * g + 2)
                    for m in range(FK):
                        mm = turn(psum[:, DN + m // 4, (m % 4) * P:(m % 4 + 1) * P], gus[:, m * P:(m + 1) * P], P)
                        if m % 4 == 3:
                            mm.then_inc(S("turned"), 1)
                    combine(g)
                    pe.wait_ge(S("pw_ready"), g + 1)
                    for i, (t0, n) in enumerate(TILES):
                        mm = turn(psum[:, PTB, t0:t0 + n], pw[0:n, i, :], n)
                    mm.then_inc(S("pt_done"), 1)
                    pe.wait_ge(S("hT_ready"), 2 * g + 2)
                    for c in range(DN_CHUNKS):
                        pe.wait_ge(S(f"w_landed{GU_CHUNKS + c}"), 16 * e + 16)
                        for hf in range(2):
                            for k in range(2):
                                base = (GU_CHUNKS + c) * CHUNK + k * D + hf * 512
                                mm = pe.matmul(psum[64 * k:64 * k + 64, DN + hf, :], hT[:, 2 * c + k, :], ring[:, base:base + 512],
                                               start=(c == 0), stop=(c == DN_CHUNKS - 1))
                        mm.then_inc(S("chunks_used"), 1)
            blocks = pe.value_load(cum[0:1, NE:NE + 1], min_val=1, max_val=NE * MAXB)
            combine(blocks)

        @block.scalar
        def _(act):
            do = Order(act, "act_order")

            def by_tile(x):
                return x.rearrange("(j g) s -> j (g s)", g=2)

            act.dma_start(vecs[0:8, :], a["norm_mix"][0].rearrange("(k p) -> k p", p=P)).then_inc(S("vecs_landed"), 16)
            act.dma_start(vecs[8:12, :], a["s5_d"][0].rearrange("(k p) -> k p", p=P)).then_inc(S("vecs_landed"), 16)
            act.dma_start(vecs[12:16, :], a["ml_gn"][0].rearrange("(k p) -> k p", p=P)).then_inc(S("vecs_landed"), 16)
            for n, x in ((A_RE, a["s5_a_re"][0]), (A_IM, a["s5_a_im"][0]), (H0R, a["state_s5_re"][0, 0]), (H0I, a["state_s5_im"][0, 0])):
                act.dma_start(prm[:, n, :], by_tile(x)).then_inc(S("prm_landed"), 16)
            act.dma_start(prm[:, LDT, 0:2], a["s5_log_dt"][0].rearrange("(j g) -> j g", g=2)).then_inc(S("prm_landed"), 16)
            act.wait_ge(S("wg_zero"), 1)
            act.dma_start(wg[:, :, 0:H], w_in[:, :, GATE0:GATE0 + H]).then_inc(S("wg_landed"), 16)
            act.dma_start(wg[:, :, 32:32 + H], w_in[:, :, GATE0 + H:GATE0 + 2 * H]).then_inc(S("wg_landed"), 16)
            for i, (t0, n) in enumerate(TILES):
                act.wait_ge(S(f"x_landed{i}"), 16)
                nc.scalar.activation(xn[0:n, i, :], acc[0:n, i, :], ACT.Square, accum_out=st[0:n, i:i + 1]).then_inc(S("ss"), 1)
            for i, (t0, n) in enumerate(TILES):
                act.wait_ge(S("ms"), i + 1)
                nc.scalar.activation(st[0:n, 6 + i:7 + i], st[0:n, 3 + i:4 + i], ACT.Sqrt).then_inc(S("rms"), 1)
            act.dma_start(cst2, a["consts"][:, C_KEEP:C_ALL]).then_inc(S("cst2_landed"), 16)
            for k, x in enumerate((a["s5_c_re"][0], a["s5_c_im"][0])):
                act.dma_start(cnat[:, k], x.rearrange("g c s -> (g c) s").rearrange("(q r) s -> r q s", r=P)).then_inc(S("cnat_landed"), 16)
            for k, x in enumerate((a["s5_b_re"][0], a["s5_b_im"][0])):
                act.dma_start(bnat[:, k], x.rearrange("g s c -> (g s) c").rearrange("(j r) c -> r j c", r=P)).then_inc(S("bnat_landed"), 16)
            act.dma_start(bcol[0:H, 0:1], a["b_ig"][0].rearrange("(h o) -> h o", o=1)).then_inc(S("bcol_landed"), 16)
            act.dma_start(bcol[32:32 + H, 0:1], a["b_fg"][0].rearrange("(h o) -> h o", o=1)).then_inc(S("bcol_landed"), 16)
            act.dma_start(bcol[0:H, 1:2], a["state_ml_m"][0, 0].rearrange("(h o) -> h o", o=1)).then_inc(S("bcol_landed"), 16)
            act.dma_start(btmp, a["b_gate_up"][0].rearrange("e (m p) -> (e m) p", p=P).rearrange("(q r) p -> r q p", r=P)).then_inc(S("btmp_landed"), 16)
            act.dma_start(c0n, a["state_ml_C"][0, 0].rearrange("h v k -> v h k")).then_inc(S("c0_landed"), 16)
            act.dma_start(n0n, a["state_ml_n"][0, 0]).then_inc(S("c0_landed"), 16)
            act.wait_ge(S("prm_landed"), 80)
            nc.scalar.activation(prm[:, LDT, 2:4], prm[:, LDT, 0:2], ACT.Exp).then_inc(S("dt_ready"), 1)
            act.wait_ge(S("dar"), 1)
            nc.scalar.activation(prm[:, MAG, :], prm[:, X0, :], ACT.Exp).then_inc(S("mag"), 1)
            act.wait_ge(S("reduced"), 1)
            nc.scalar.activation(prm[:, SIN, :], prm[:, RED, :], ACT.Sin).then_inc(S("sincos"), 1)
            nc.scalar.activation(prm[:, COS, :], prm[:, X2, :], ACT.Sin).then_inc(S("sincos"), 1)

            def evac(j, dst, func=ACT.Copy, scale=1.0):
                act.wait_ge(S("pj_done"), j + 1)
                nc.scalar.activation(dst, PJ[j % 2][:, 0:T], func, scale=scale).then_inc(S(f"pj_free{j % 2}"), 1)

            def publish(j, name):
                act.wait_ge(S("pj_free0"), j // 2 + 1)
                act.wait_ge(S("pj_free1"), (j + 1) // 2)
                act.sem_inc(S(name), 1)

            def gate_rows(_):
                act.wait_ge(S("gate_mm"), 1)
                act.wait_ge(S("bcol_landed"), 48)
                do(nc.scalar.activation(rows[R_IG], psum[0:H, 5, 0:T], ACT.Identity, bias=bcol[0:H, 0:1]))
                do(nc.scalar.activation(rows[R_LF], psum[32:32 + H, 5, 0:T], ACT.Identity, bias=bcol[32:32 + H, 0:1]))
                act.sem_inc(S("gate_rows"), 1)
                act.wait_ge(S("fabs"), 1)
                do(nc.scalar.activation(rows[R_A], rows[R_B], ACT.Exp, scale=-1.0))
                nc.scalar.activation(rows[R_AL], rows[R_A], ACT.Ln, bias=1.0).then_inc(S("softplus"), 1)

            def biases(_):
                act.wait_ge(S("bgT"), 1)
                nc.scalar.copy(flat(bg[:, :, :, :]), psum[:, 3, :]).then_inc(S("bg_ready"), 1)

            def state_in(_):
                act.wait_ge(S("c0T"), 1)
                do(nc.scalar.copy(cn0[:, :, 0:HD], cut(psum[:, 6, :], H, HD)))
                nc.scalar.copy(cn0[:, :, HD], psum[:, 7, 0:H]).then_inc(S("cn0_ready"), 1)

            def c_matrix(_):
                act.wait_ge(S("cT"), 1)
                do(nc.scalar.copy(flat(ctt[:, 0]), psum[:, 6, :]))
                nc.scalar.mul(flat(ctt[:, 1]), psum[:, 7, :], -1.0).then_inc(S("ctt_ready"), 1)

            def b_matrix(_):
                act.wait_ge(S("bT"), 1)
                act.wait_ge(S("btz_zero"), 1)
                for k in range(2):
                    for q in range(4):
                        s = slice(32 * q, 32 * q + 32)
                        do(nc.scalar.copy(btz[s, k, q:NJ:4, :], cut(psum[s, 6 + k, :], 4, P)))
                act.sem_inc(S("btz_ready"), 1)

            def row_columns(_):
                act.wait_ge(S("wexp"), 1)
                do(nc.scalar.activation(rows[R_WI], rows[R_WI], ACT.Exp))
                nc.scalar.activation(rows[R_WE], rows[R_WE], ACT.Exp).then_inc(S("rows_ready"), 1)
                act.wait_ge(S("cols_mm"), 1)
                do(nc.scalar.copy(wcol[:, 0:2], cut(psum[0:CH, 2, 0:2 * NC * H], 2, NC, H)))
                do(nc.scalar.activation(wcol[:, 2], cut(psum[0:CH, 2, 2 * NC * H:3 * NC * H], NC, H), ACT.Exp, scale=-1.0))
                nc.scalar.copy(flat(dec), psum[:, 3, 0:H * NC]).then_inc(S("cols_ready"), 1)

            def decay_matrix(h):
                act.wait_ge(S("dm_read"), h + 1)
                nc.scalar.activation(wt[:, h], wt[:, h], ACT.Exp).then_inc(S("wt_ready"), 1)

            def natural(c):
                for i in (2 * c, 2 * c + 1):
                    act.wait_ge(S("nat_done"), i + 1)
                    if i == 1:
                        act.wait_ge(S("vn_ones"), 1)
                    dst = kn[:, c] if i % 2 == 0 else vn[:, c, :, 0:HD]
                    nc.scalar.copy(dst, cut(psum[0:CH, 6 + i % 2, :], H, HD)).then_inc(S("nat_read"), 1)

            def chunk(c):
                act.wait_ge(S("var_ready"), c + 1)
                nc.scalar.activation(den[0:CH, H:2 * H], den[0:CH, 0:H], ACT.Sqrt).then_inc(S("std_ready"), 1)

            def states_out(s):
                act.wait_ge(S("co_done"), s + 1)
                nc.scalar.copy(flat(stage[s][0]), psum[:, 6, :]).then_inc(S("co_read"), 1)
                nc.scalar.copy(stage[s][1], psum[0:H, 7, 0:P]).then_inc(S("co_read"), 1)
                act.wait_ge(S("co_read"), 2 * s + 2)
                o = 4 + 5 * s
                act.dma_start(out[o][0, 0].rearrange("h v k -> v h k"), stage[s][0]).then_inc(S("states_stored"), 16)
                act.dma_start(out[o + 1][0, 0], stage[s][1]).then_inc(S("states_stored"), 16)
                last = (TP if s == 0 else T) - 1
                act.dma_start(out[o + 2][0, 0].rearrange("(h o) -> h o", o=1), rows[R_M][:, last:last + 1]).then_inc(S("states_stored"), 16)

            def s5_out_states(_):
                act.wait_ge(S("finT"), 1)
                do(nc.scalar.copy(stage5, cut(psum[0:NJ, 2, :], 4, P)))
                for n, o in enumerate((2, 3, 7, 8)):
                    act.dma_start(by_tile(out[o][0, 0]), stage5[:, n, :]).then_inc(S("states_stored"), 16)

            steps = dict(gate_rows=gate_rows, biases=biases, state_in=state_in, c_matrix=c_matrix, b_matrix=b_matrix,
                         row_columns=row_columns, decay_matrix=decay_matrix, natural=natural, chunk=chunk,
                         states_out=states_out, s5_out_states=s5_out_states)

            for j in range(T_GLU):
                if j < 4:
                    evac(j, uT[:, j, :])
                elif j < 8:
                    evac(j, qT[:, j - 4, :], scale=HD ** -0.5)
                elif j < 12:
                    evac(j, kT[:, j - 8, :])
                elif j < 16:
                    evac(j, vT[:, j - 12, :])
                elif j < 20:
                    if j == 16:
                        act.wait_ge(S("dm_done"), H)
                    evac(j, oT[:, j - 16, :], ACT.Sigmoid)
                elif j < 28:
                    evac(j, gS[:, j - 20, :], ACT.Sigmoid)
                else:
                    evac(j, gM[:, j - 28, :], ACT.Sigmoid)
                if j == 3:
                    publish(j, "u_ready")
                if j == 15:
                    publish(j, "qkv_ready")
                if j == 35:
                    publish(j, "gates_ready")
                if j == 30:
                    for q in range(4):
                        act.wait_ge(S("y_read"), q + 1)
                        nc.scalar.activation(uT[:, q, :], uT[:, q, :], ACT.Gelu_apprx_tanh).then_inc(S("gelu_ready"), 1)
                for step, n in plan[j]:
                    if step in steps:
                        steps[step](n)
            for i in range(16):
                j = T_GLU + i
                if i % 2 == 1:
                    if i > 1:
                        act.wait_ge(S("glu_done"), i // 2)
                    evac(j, gtmp, ACT.Sigmoid)
                for step, n in plan[j]:
                    if step in steps:
                        steps[step](n)

            for i, (t0, n) in enumerate(TILES):
                act.wait_ge(S("x1_ready"), i + 1)
                nc.scalar.activation(square1[0:n, i, :], acc[0:n, i, :], ACT.Square, accum_out=st[0:n, i:i + 1]).then_inc(S("ss"), 1)
                act.wait_ge(S("ms"), 4 + i)
                nc.scalar.activation(st[0:n, 6 + i:7 + i], st[0:n, 3 + i:4 + i], ACT.Sqrt).then_inc(S("rms"), 1)
            for i, (t0, n) in enumerate(TILES):
                act.wait_ge(S("xm_ready"), i + 1)
                nc.scalar.copy(parts[0:n, 0, i, :], xm[0:n, i, :]).then_inc(S("rounded"), 1)
                act.wait_ge(S("rest"), i + 1)
                nc.scalar.copy(parts[0:n, 1, i, :], gus[0:n, :]).then_inc(S("rounded"), 1)
            for i, (t0, n) in enumerate(TILES):
                act.wait_ge(S("top_ready"), i + 1)
                _, t8, _, f8 = (x[0:n] for x in top[i])
                nc.scalar.activation(f8[:, 4:8], t8[:, 0:4], ACT.Exp, bias=f8[:, 8:9], accum_out=f8[:, 9:10]).then_inc(S("top_exp"), 1)
            act.wait_ge(S("cum_ready"), 1)
            with act.Fori(0, NE) as e:
                first = act.value_load(cum[0:1, bass.ds(e, 1)], min_val=0, max_val=NE * MAXB)
                end = act.value_load(cum[0:1, bass.ds(e + 1, 1)], min_val=1, max_val=NE * MAXB)
                with act.Fori(first, end) as g:
                    act.wait_ge(S("chunks_used"), CHUNKS * g + (CHUNKS + GU_CHUNKS))
                    act.wait_ge(S("turned"), 2 * g + 2)
                    for hf in range(2):
                        nc.scalar.copy(gus[:, hf * 512:(hf + 1) * 512], psum[:, GU + hf, :]).then_inc(S("gus_ready"), 1)
                    for hf in range(2):
                        act.wait_ge(S("clamped"), 2 * g + hf + 1)
                        nc.scalar.activation(sg[:, 4 * hf:4 * hf + 4, :], hb[:, 4 * hf:4 * hf + 4, 0, :], ACT.Sigmoid,
                                             scale=ALPHA).then_inc(S("sg_ready"), 1)
                    act.wait_ge(S("chunks_used"), CHUNKS * g + 2 * CHUNKS)
                    act.wait_ge(S("combined"), 6 * g + 6)
                    for hf in range(2):
                        nc.scalar.copy(osb[:, hf * 512:(hf + 1) * 512], psum[:, DN + hf, :]).then_inc(S("osb_ready"), 1)
            for i, (t0, n) in enumerate(TILES):
                act.wait_ge(S("acc_ready"), 1)
                nc.scalar.activation(square2[0:n, i, :], acc[0:n, i, :], ACT.Square, accum_out=st[0:n, i:i + 1]).then_inc(S("ss"), 1)
                act.wait_ge(S("ms"), 7 + i)
                nc.scalar.activation(st[0:n, 6 + i:7 + i], st[0:n, 3 + i:4 + i], ACT.Sqrt).then_inc(S("rms"), 1)
            act.wait_ge(S("states_stored"), 160)

        def angles(eng, do, part):
            js = slice(part * NJ // 2, (part + 1) * NJ // 2)
            c, s, tmp = ct[:, js, :], sn[:, js, :], ttmp[part]
            do(eng.tensor_copy(c[:, :, 0], pcol[:, M_COS, js]))
            do(eng.tensor_copy(s[:, :, 0], pcol[:, M_SIN, js]))
            m = 1
            while m < TP:
                cm = c[:, :, m - 1:m].to_broadcast([P, NJ // 2, m])
                sm_ = s[:, :, m - 1:m].to_broadcast([P, NJ // 2, m])
                old, new = slice(0, m), slice(m, 2 * m)
                do.start(eng.tensor_tensor(c[:, :, new], c[:, :, old], cm, ALU.mult))
                do.start(eng.tensor_tensor(s[:, :, new], s[:, :, old], cm, ALU.mult))
                do(eng.tensor_tensor(tmp[:, :, 0:m], s[:, :, old], sm_, ALU.mult))
                do(eng.tensor_tensor(c[:, :, new], c[:, :, new], tmp[:, :, 0:m], ALU.subtract))
                do(eng.tensor_tensor(tmp[:, :, 0:m], c[:, :, old], sm_, ALU.mult))
                do(eng.tensor_tensor(s[:, :, new], s[:, :, new], tmp[:, :, 0:m], ALU.add))
                m *= 2
            do.start(eng.tensor_copy(c[:, :, TP:T], c[:, :, 0:TS]))
            do(eng.tensor_copy(s[:, :, TP:T], s[:, :, 0:TS]))

        @block.gpsimd
        def _(pool):
            do = Order(pool, "pool_order")
            nc.gpsimd.memset(wg, 0.0).then_inc(S("wg_zero"), 1)
            nc.gpsimd.memset(btz, 0.0).then_inc(S("btz_zero"), 1)
            nc.gpsimd.memset(bpad, 0.0).then_inc(S("btz_zero"), 1)
            pool.wait_ge(S("cnat_landed"), 32)
            pool.wait_ge(S("cst2_landed"), 16)
            for k in range(2):
                for par in range(2):
                    c = C_PAR - C_KEEP + par
                    do(nc.gpsimd.tensor_scalar(cpad[:, k, :, par, :], cnat[:, k], cst2[:, c:c + 1], None, ALU.mult))
            pool.sem_inc(S("cpad_ready"), 1)
            pool.wait_ge(S("pcol_ready"), 1)
            pool.wait_ge(S("xnT_ready"), 3)
            angles(nc.gpsimd, do, 1)
            pool.sem_inc(S("table_ready"), 1)

            def s5_in(j):
                b = j % 2
                C, Sn = ct[:, j, :], sn[:, j, :]
                if j == 0:
                    pool.wait_ge(S("table_ready"), 2)
                pool.wait_ge(S("g_ready"), j + 1)
                if j >= 2:
                    pool.wait_ge(S("y_done"), j - 1)
                tt = nc.gpsimd.tensor_tensor
                do.start(tt(ptmp[:, 0, :], Sn, zz[:, b, 1, :], ALU.mult))
                do.start(tt(hh[:, b, 0, :], C, zz[:, b, 0, :], ALU.mult))
                do.start(tt(ptmp[:, 1, :], Sn, zz[:, b, 0, :], ALU.mult))
                do(tt(hh[:, b, 1, :], C, zz[:, b, 1, :], ALU.mult))
                do(tt(hh[:, b, 0, :], hh[:, b, 0, :], ptmp[:, 0, :], ALU.subtract))
                tt(hh[:, b, 1, :], hh[:, b, 1, :], ptmp[:, 1, :], ALU.add).then_inc(S("h_ready"), 1)
                pool.wait_ge(S("h_ready"), j + 1)
                nc.gpsimd.tensor_copy(fin[:, 0:2, j], hh[:, b, :, TP - 1]).then_inc(S("fin_ready"), 1)
                nc.gpsimd.tensor_copy(fin[:, 2:4, j], hh[:, b, :, T - 1]).then_inc(S("fin_ready"), 1)

            def natural(c):
                if c == 0:
                    nc.gpsimd.memset(vn[:, :, :, HD:HD + 1], 1.0).then_inc(S("vn_ones"), 1)

            def chunk(c):
                if c == 0:
                    pool.wait_ge(S("nat_read"), 2 * NC)
                    pool.wait_ge(S("vn_ones"), 1)
                    pool.wait_ge(S("cols_ready"), 1)
                    pool.wait_ge(S("y_done"), NJ)
                else:
                    pool.wait_ge(S("u_done"), c)
                nc.gpsimd.tensor_tensor(vw, vn[:, c], wcol[:, 1, c, :][:, :, None].to_broadcast([CH, H, HD + 1]),
                                        ALU.mult).then_inc(S("vw_ready"), 1)

            steps = dict(s5_in=s5_in, natural=natural, chunk=chunk)
            for j in range(T_ML):
                for step, n in plan[j]:
                    if step in steps:
                        steps[step](n)
            pool.wait_ge(S("group_used"), 28)
            pool.wait_ge(S("cn_ready"), NC)
            pool.wait_ge(S("hT_read"), NC)
            pool.wait_ge(S("co_read"), 4)
            for q in range(3):
                do(nc.gpsimd.memset(parts[64:128, q, 2, :], 0.0))
            do(nc.gpsimd.memset(tab[:, :, 0:3], -1.0))
            do(nc.gpsimd.memset(tab[:, :, 3:6], 0.0))
            pool.sem_inc(S("tab_set"), 1)
            for i, (t0, n) in enumerate(TILES):
                pool.wait_ge(S("rounded"), 2 * i + 1)
                nc.gpsimd.tensor_tensor(gus[0:n, :], xm[0:n, i, :], parts[0:n, 0, i, :], ALU.subtract).then_inc(S("rest"), 1)
                pool.wait_ge(S("rounded"), 2 * i + 2)
                do(nc.gpsimd.tensor_tensor(gus[0:n, :], gus[0:n, :], parts[0:n, 1, i, :], ALU.subtract))
                do(nc.gpsimd.tensor_copy(parts[0:n, 2, i, :], gus[0:n, :]))
                pool.sem_inc(S("parts_ready"), 1)
            do(nc.gpsimd.memset(osb, 0.0))
            do(nc.gpsimd.memset(pt, 0.0))
            pool.sem_inc(S("osb_ready"), 2)
            pool.sem_inc(S("pt_ready"), 1)
            pool.sem_inc(S("cur_set"), 1)
            for name, n in (("added", 2), ("gus_ready", 2), ("turned", 2), ("gathered", 1), ("pt_done", 1), ("chunks_used", CHUNKS)):
                pool.sem_inc(S(name), n)
            pool.wait_ge(S("tab_ready"), 3)
            pool.wait_ge(S("cum_ready"), 1)

            with pool.Fori(0, NE) as e:
                first = pool.value_load(cum[0:1, bass.ds(e, 1)], min_val=0, max_val=NE * MAXB)
                end = pool.value_load(cum[0:1, bass.ds(e + 1, 1)], min_val=1, max_val=NE * MAXB)
                pool.wait_ge(S("cur_set"), first + e + 1)
                pool.sem_inc(S("pool_go"), 1)
                nc.gpsimd.tensor_copy(cur, tab[:, bass.ds(e, 1), :].rearrange("p a b -> p (a b)")).then_inc(S("cur_set"), 1)
                with pool.Fori(first, end) as g:
                    ts = nc.gpsimd.tensor_scalar
                    pool.wait_ge(S("cur_set"), g + e + 2)
                    pool.wait_ge(S("gathered"), g + 1)
                    pool.sem_inc(S("pool_go"), 1)
                    for i in range(3):
                        ts(pb[:, i, :], cst[:, C_SLOT:C_SLOT + SLOT], cur[:, i:i + 1], None, ALU.is_equal).then_inc(S("pool_p"), 1)
                    pool.wait_ge(S("pool_p"), 3 * g + 3)
                    pool.sem_inc(S("p_ready"), 1)
                    pool.wait_ge(S("pt_done"), g + 1)
                    pool.sem_inc(S("pool_go"), 1)
                    for i in range(3):
                        ts(pw[:, i, :], cst[:, C_SLOT:C_SLOT + P], cur[:, i:i + 1], cur[:, 3 + i:4 + i],
                           ALU.is_equal, ALU.mult).then_inc(S("pool_pw"), 1)
                    pool.wait_ge(S("pool_pw"), 3 * g + 3)
                    pool.sem_inc(S("pw_ready"), 1)
                    ts(cur[:, 0:3], cur[:, 0:3], float(SLOT), None, ALU.subtract).then_inc(S("cur_set"), 1)
            pool.sem_inc(S("p_ready"), 1)

        @block.vector
        def _(dve):
            v = nc.vector
            do = Order(dve, "dve_order")

            def inverse_rms(i, n, k):
                dve.wait_ge(S("ss"), 3 * k + i + 1)
                v.tensor_scalar(st[0:n, 3 + i:4 + i], st[0:n, i:i + 1], 1.0 / D, EPS, ALU.mult, ALU.add).then_inc(S("ms"), 1)
                dve.wait_ge(S("rms"), 3 * k + i + 1)
                do(v.reciprocal(st[0:n, 9 + i:10 + i], st[0:n, 6 + i:7 + i]))
                return st[0:n, 9 + i:10 + i]

            for i, (t0, n) in enumerate(TILES):
                inv = inverse_rms(i, n, 0)
                v.tensor_scalar(xn[0:n, i, :], acc[0:n, i, :], inv, None, ALU.mult).then_inc(S("xn_ready"), 1)
            dve.wait_ge(S("vcT"), 1)
            v.tensor_copy(vc[:, :], psum[:, 0, 0:16]).then_inc(S("vc_ready"), 1)
            dve.wait_ge(S("vc_ready"), 1)
            for i, (t0, n) in enumerate(TILES):
                dve.wait_ge(S("xT"), i + 1)
                src = cut(flat(psum[:, 2 + 2 * i:4 + 2 * i, :]), DK, P)[:, :, 0:n]
                v.tensor_tensor(xnT[:, :, t0:t0 + n], src, vc[:, 0:DK][:, :, None].to_broadcast([P, DK, n]),
                                ALU.mult).then_inc(S("xnT_ready"), 1)

            def q(k):
                return prm[:, k, :]
            dve.wait_ge(S("dt_ready"), 1)
            dt = prm[:, LDT, 2:4][:, :, None].to_broadcast([NJ, 2, S5P])
            v.tensor_tensor(cut(q(X0), 2, S5P), cut(q(A_RE), 2, S5P), dt, ALU.mult).then_inc(S("dar"), 1)
            do(v.tensor_tensor(cut(q(DAI), 2, S5P), cut(q(A_IM), 2, S5P), dt, ALU.mult))
            do(v.tensor_scalar(q(X1), q(DAI), 1.0 / TWO_PI, ROUND, ALU.mult, ALU.add))
            do(v.tensor_scalar(q(X1), q(X1), ROUND, None, ALU.subtract))
            do(v.scalar_tensor_tensor(out=q(RED), in0=q(X1), scalar=-PI2_A, in1=q(DAI), op0=ALU.mult, op1=ALU.add))
            do(v.scalar_tensor_tensor(out=q(RED), in0=q(X1), scalar=-PI2_B, in1=q(RED), op0=ALU.mult, op1=ALU.add))
            do(v.scalar_tensor_tensor(out=q(RED), in0=q(X1), scalar=-PI2_C, in1=q(RED), op0=ALU.mult, op1=ALU.add))
            do(v.tensor_scalar(q(RED), q(RED), PI_IN, -PI_IN, ALU.min, ALU.max))
            do(v.scalar_tensor_tensor(out=q(X2), in0=q(RED), scalar=-1.0, in1=q(RED), op0=ALU.mult, op1=ALU.min))
            do(v.tensor_scalar(q(X2), q(X2), TWO_PI / 4, None, ALU.add))
            dve.sem_inc(S("reduced"), 1)
            dve.wait_ge(S("sincos"), 2)
            dve.wait_ge(S("mag"), 1)
            do(v.tensor_tensor(q(X0), q(MAG), q(COS), ALU.mult))
            do(v.tensor_tensor(q(X1), q(MAG), q(SIN), ALU.mult))
            do(v.tensor_tensor(q(DEN), q(A_RE), q(A_RE), ALU.mult))
            do(v.tensor_tensor(q(X2), q(A_IM), q(A_IM), ALU.mult))
            do(v.tensor_tensor(q(DEN), q(DEN), q(X2), ALU.add))
            do(v.reciprocal(q(DEN), q(DEN)))
            do(v.tensor_scalar(q(X0), q(X0), 1.0, None, ALU.subtract))
            do(v.tensor_tensor(q(FR), q(X0), q(A_RE), ALU.mult))
            do(v.tensor_tensor(q(X2), q(X1), q(A_IM), ALU.mult))
            do(v.tensor_tensor(q(FR), q(FR), q(X2), ALU.add))
            do(v.tensor_tensor(q(FR), q(FR), q(DEN), ALU.mult))
            do(v.tensor_tensor(q(FI), q(X1), q(A_RE), ALU.mult))
            do(v.tensor_tensor(q(X2), q(X0), q(A_IM), ALU.mult))
            do(v.tensor_tensor(q(FI), q(FI), q(X2), ALU.subtract))
            do(v.tensor_tensor(q(FI), q(FI), q(DEN), ALU.mult))
            dve.sem_inc(S("prm_ready"), 1)

            def s5_columns(_):
                dve.wait_ge(S("prmT"), 1)
                v.tensor_copy(flat(pcol), psum[:, 2, 0:7 * NJ]).then_inc(S("pcol_ready"), 1)
                dve.wait_ge(S("pcol_ready"), 1)
                dve.wait_ge(S("bnat_landed"), 32)
                dve.wait_ge(S("btz_zero"), 2)
                fr = pcol[:, M_FR, :][:, :, None].to_broadcast([P, NJ, S5C])
                fi = pcol[:, M_FI, :][:, :, None].to_broadcast([P, NJ, S5C])
                for n, (f, k) in enumerate(((fr, 0), (fi, 1), (fr, 1), (fi, 0))):
                    do(v.tensor_tensor(btmp2[:, n], bnat[:, k], f, ALU.mult))
                for par in range(2):
                    s, c = slice(64 * par, 64 * par + 64), slice(S5C * par, S5C * par + S5C)
                    do(v.tensor_tensor(bpad[s, 0, :, c], btmp2[s, 0], btmp2[s, 1], ALU.subtract))
                    do(v.tensor_tensor(bpad[s, 1, :, c], btmp2[s, 2], btmp2[s, 3], ALU.add))
                dve.sem_inc(S("bpad_ready"), 1)
                angles(v, do, 0)
                dve.sem_inc(S("table_ready"), 1)

            def gate_rows(_):
                dve.wait_ge(S("gate_rows"), 1)
                R = rows
                v.scalar_tensor_tensor(out=R[R_B], in0=R[R_LF], scalar=-1.0, in1=R[R_LF], op0=ALU.mult, op1=ALU.max).then_inc(S("fabs"), 1)
                dve.wait_ge(S("softplus"), 1)
                do(v.scalar_tensor_tensor(out=R[R_LF], in0=R[R_LF], scalar=0.0, in1=R[R_AL], op0=ALU.min, op1=ALU.subtract))
                seg = cst2[0:H, C_SEG - C_KEEP:C_SEG - C_KEEP + T]
                do(v.tensor_tensor_scan(R[R_B], seg, R[R_LF], 0.0, ALU.mult, ALU.add))
                do(v.tensor_tensor_scan(R[R_M][:, 0:TP], R[R_LF][:, 0:TP], R[R_IG][:, 0:TP], 0.0, ALU.add, ALU.max))
                do(v.tensor_tensor_scan(R[R_M][:, TP:T], R[R_LF][:, TP:T], R[R_IG][:, TP:T], bcol[0:H, 1:2], ALU.add, ALU.max))
                do(v.tensor_tensor(R[R_A], R[R_IG], R[R_B], ALU.subtract))
                do(v.tensor_tensor(R[R_AL], R[R_B], R[R_M], ALU.subtract))
                al, wi, m = by_chunk(R_AL), by_chunk(R_WI), by_chunk(R_M)
                do(v.tensor_copy(wi[:, 0, :], al[:, 0, :]))
                do(v.tensor_tensor(wi[:, 1:NCP, :], al[:, 1:NCP, :], m[:, 0:NCP - 1, CH - 1:CH].to_broadcast([H, NCP - 1, CH]), ALU.add))
                do(v.tensor_scalar(wi[:, NCP, :], al[:, NCP, :], bcol[0:H, 1:2], None, ALU.add))
                do(v.tensor_tensor(by_chunk(R_WE), by_chunk(R_A), al[:, :, CH - 1:CH].to_broadcast([H, NC, CH]), ALU.add))
                dve.sem_inc(S("wexp"), 1)

            def state_in(_):
                pass

            def decay_matrix(h):
                dve.wait_ge(S("dm_done"), h + 1)
                mask = cst2[0:CH, C_CAUSAL - C_KEEP:C_CAUSAL - C_KEEP + CH][:, None, :].to_broadcast([CH, NC, CH])
                v.tensor_tensor(wt[:, h], cut(psum[0:CH, 6 + h % 2, 0:T], NC, CH), mask, ALU.add).then_inc(S("dm_read"), 1)

            def s5_in(j):
                b = j % 2
                C, Sn, br, bi = ct[:, j, :], sn[:, j, :], psum[:, 2, 0:T], psum[:, 3, 0:T]
                if j == 0:
                    dve.wait_ge(S("table_ready"), 2)
                dve.wait_ge(S("bu_done"), j + 1)
                if j >= 2:
                    dve.wait_ge(S("h_ready"), j - 1)
                do.start(v.tensor_tensor(dtmp[:, 0, :], Sn, bi, ALU.mult))
                do.start(v.tensor_tensor(zz[:, b, 0, :], C, br, ALU.mult))
                do.start(v.tensor_tensor(dtmp[:, 1, :], Sn, br, ALU.mult))
                v.tensor_tensor(zz[:, b, 1, :], C, bi, ALU.mult).then_inc(S("bu_read"), 1)
                do.wait()
                do.start(v.tensor_tensor(zz[:, b, 0, :], zz[:, b, 0, :], dtmp[:, 0, :], ALU.add))
                dve.wait_ge(S("bu_read"), j + 1)
                do(v.tensor_tensor(zz[:, b, 1, :], zz[:, b, 1, :], dtmp[:, 1, :], ALU.subtract))
                for k in range(2):
                    mag = pcol[:, M_MAG, j:j + 1]
                    zp, zs = zz[:, b, k, 0:TP], zz[:, b, k, TP:T]
                    do.start(v.tensor_tensor_scan(zp, mag.to_broadcast([P, TP]), zp, 0.0, ALU.mult, ALU.add))
                    do.start(v.tensor_tensor_scan(zs, mag.to_broadcast([P, TS]), zs, pcol[:, M_H0R + k, j:j + 1], ALU.mult, ALU.add))
                do.wait()
                dve.sem_inc(S("g_ready"), 1)

            def s5_out(j):
                t = j // 4
                if j % 4 == 3:
                    dve.wait_ge(S("y_done"), j + 1)
                    do(v.scalar_tensor_tensor(out=uT[:, t, :], in0=uT[:, t, :], scalar=vc[:, 8 + t:9 + t], in1=psum[:, 4, 0:T],
                                              op0=ALU.mult, op1=ALU.add))
                    dve.sem_inc(S("y_read"), 1)

            def scores(h):
                dve.wait_ge(S("sc_done"), h + 1)
                dve.wait_ge(S("wt_ready"), h + 1)
                v.tensor_tensor(flat(wt[:, h]), psum[0:CH, 6 + h % 2, 0:T], flat(wt[:, h]), ALU.mult).then_inc(S("st_ready"), 1)

            def pairs(ap):
                return ap.rearrange("p (b h) v -> p b h v", b=2)

            def banks(b, n):
                return psum[0:n, b:b + 2, 0:2 * (HD + 1)].rearrange("p b (h v) -> p b h v", h=2)

            def chunk(c):
                dve.wait_ge(S("a_done"), c + 1)
                if c == 0:
                    dve.wait_ge(S("h_ready"), NJ)
                    dve.wait_ge(S("y_done"), NJ)
                    do(v.tensor_copy(pairs(num), banks(2, CH)))
                else:
                    dve.wait_ge(S("b_done"), c)
                    wi = pairs(wcol[:, 0, c, :][:, :, None].to_broadcast([CH, H, HD + 1]))
                    do(v.tensor_tensor(pairs(num), banks(4, CH), wi, ALU.mult))
                    do(v.tensor_tensor(pairs(num), pairs(num), banks(2, CH), ALU.add))
                dve.wait_ge(S("u_done"), c + 1)
                new = cn[:, (c + 1) % 2]
                if c == 0:
                    do(v.tensor_copy(pairs(new), banks(6, P)))
                else:
                    old = cn[:, c % 2] if c < NCP else cn0
                    for h in range(H):
                        do.start(v.scalar_tensor_tensor(out=new[:, h, :], in0=old[:, h, :], scalar=dec[:, h, c:c + 1],
                                                        in1=psum[:, 6 + h // 2, (h % 2) * 129:(h % 2) * 129 + 129],
                                                        op0=ALU.mult, op1=ALU.add))
                    do.wait()
                dve.sem_inc(S("cn_ready"), 1)
                d4 = den[0:CH, 0:H]
                do(v.scalar_tensor_tensor(out=d4, in0=num[:, :, HD], scalar=-1.0, in1=num[:, :, HD], op0=ALU.mult, op1=ALU.max))
                do(v.tensor_tensor(d4, d4, wcol[:, 2, c, :], ALU.max))
                do(v.reciprocal(d4, d4))
                if c > 0:
                    dve.wait_ge(S("hT_done"), c)
                do(v.tensor_tensor(hn, num[:, :, 0:HD], d4[:, :, None].to_broadcast([CH, H, HD]), ALU.mult))
                for h in range(H):
                    do.start(v.bn_stats(bns[0:CH, h, :], hn[:, h, :]))
                do.wait()
                for h in range(H):
                    do.start(v.bn_aggr(mv[0:CH, h, :], bns[0:CH, h, :]))
                do.wait()
                v.tensor_scalar(d4, mv[0:CH, :, 1], EPS, None, ALU.add).then_inc(S("var_ready"), 1)
                dve.wait_ge(S("std_ready"), c + 1)
                s4 = den[0:CH, H:2 * H]
                do(v.reciprocal(s4, s4))
                for h in range(H):
                    do.start(v.tensor_scalar(hn[:, h, :], hn[:, h, :], mv[0:CH, h, 0:1], s4[:, h:h + 1], ALU.subtract, ALU.mult))
                do.wait()
                dve.sem_inc(S("hn_ready"), 1)

            def turn(c):
                dve.wait_ge(S("hT_done"), c + 1)
                for h in range(H):
                    o = oT[:, h, c * CH:(c + 1) * CH]
                    do.start(v.scalar_tensor_tensor(out=o, in0=psum[:, 2, h * CH:(h + 1) * CH], scalar=vc[:, 12 + h:13 + h],
                                                    in1=o, op0=ALU.mult, op1=ALU.mult))
                do.wait()
                dve.sem_inc(S("hT_read"), 1)

            steps = dict(s5_columns=s5_columns, gate_rows=gate_rows, decay_matrix=decay_matrix,
                         s5_in=s5_in, s5_out=s5_out, scores=scores, chunk=chunk, turn=turn)

            def glu(p):
                j = T_GLU + 2 * p
                if p == 0:
                    dve.wait_ge(S("gates_ready"), 1)
                dve.wait_ge(S("pj_done"), j + 1)
                dve.wait_ge(S("pj_free1"), j // 2 + 1)
                v.tensor_tensor(gtmp, PJ[0][:, 0:T], gtmp, ALU.mult).then_inc(S("pj_free0"), 1)
                dve.wait_ge(S("pj_free0"), j // 2 + 1)
                v.tensor_tensor(gS[:, p, :], gS[:, p, :], gtmp, ALU.mult).then_inc(S("glu_done"), 1)

            for j in range(T_ML):
                for step, n in plan[j]:
                    if step in steps:
                        steps[step](n)
                if j >= T_GLU and j % 2 == 1:
                    glu((j - T_GLU) // 2)
            dve.wait_ge(S("glu_done"), 8)
            for i in range(DK):
                j = T_ML + i
                dve.wait_ge(S("pj_done"), j + 1)
                if i > 0:
                    dve.wait_ge(S("mix_ready"), i)
                v.tensor_tensor(gtmp, PJ[j % 2][:, 0:T], gM[:, i, :], ALU.mult).then_inc(S(f"pj_free{j % 2}"), 1)
                dve.wait_ge(S(f"pj_free{j % 2}"), j // 2 + 1)
                v.tensor_tensor(gS[:, i, :], gS[:, i, :], gtmp, ALU.add).then_inc(S("mix_ready"), 1)
            dve.wait_ge(S("res_landed"), 48)
            for gg in range(4):
                for i, (t0, n) in enumerate(TILES):
                    j = T_OUT + 3 * gg + i
                    dve.wait_ge(S("pj_done"), j + 1)
                    x = acc[0:n, i, 256 * gg:256 * gg + 256]
                    v.tensor_tensor(x, x, PJ[j % 2][0:n, 0:256], ALU.add).then_inc(S(f"pj_free{j % 2}"), 1)
                    dve.wait_ge(S(f"pj_free{j % 2}"), j // 2 + 1)
                    if gg == 3:
                        dve.sem_inc(S("x1_ready"), 1)

            dve.wait_ge(S("nmb_landed"), 16)
            for i, (t0, n) in enumerate(TILES):
                inv = inverse_rms(i, n, 1)
                v.scalar_tensor_tensor(out=xm[0:n, i, :], in0=acc[0:n, i, :], scalar=inv, in1=nmb[0:n, :],
                                       op0=ALU.mult, op1=ALU.mult).then_inc(S("xm_ready"), 1)
            for i, (t0, n) in enumerate(TILES):
                dve.wait_ge(S("xmT"), i + 1)
                src = cut(flat(psum[:, 2 + 2 * i:4 + 2 * i, :]), DK, P)[:, :, 0:n]
                v.tensor_copy(xnT[:, :, t0:t0 + n], src).then_inc(S("xmT_ready"), 1)
            exps = cst[:, C_EXP:C_EXP + NE]
            dve.wait_ge(S("wrt_landed"), 32)
            for i, (t0, n) in enumerate(TILES):
                lg, t8, i8, f8 = (x[0:n] for x in top[i])
                dve.wait_ge(S("logits"), i + 1)
                do(v.tensor_tensor(lg, psum[0:n, i, 0:NE], brt[0:n, :], ALU.add))
                do(v.max(t8, lg))
                do(v.max_index(i8, t8, lg))
                do(v.tensor_copy(f8[:, 0:TOPK], i8[:, 0:TOPK]))
                do(v.tensor_scalar(f8[:, 8:9], t8[:, 0:1], -1.0, None, ALU.mult))
                dve.sem_inc(S("top_ready"), 1)
                m = msk[0:n, i, :]
                do(v.tensor_scalar(m, exps[0:n, :], f8[:, 0:1], None, ALU.is_equal))
                for k in range(1, TOPK):
                    do(v.scalar_tensor_tensor(out=m, in0=exps[0:n, :], scalar=f8[:, k:k + 1], in1=m, op0=ALU.is_equal, op1=ALU.add))
                dve.sem_inc(S("mask_ready"), 1)
            dve.wait_ge(S("tab_set"), 1)
            for i, (t0, n) in enumerate(TILES):
                lg, t8, i8, f8 = (x[0:n] for x in top[i])
                dve.wait_ge(S("top_exp"), i + 1)
                do(v.reciprocal(f8[:, 10:11], f8[:, 9:10]))
                do(v.tensor_scalar(f8[:, 11:15], f8[:, 4:8], f8[:, 10:11], None, ALU.mult))
                for k in range(TOPK):
                    dst = tk[0:n, :] if k else lg
                    do(v.tensor_scalar(dst, exps[0:n, :], f8[:, k:k + 1], f8[:, 11 + k:12 + k], ALU.is_equal, ALU.mult))
                    if k:
                        do(v.tensor_tensor(lg if k < TOPK - 1 else tab[0:n, :, 3 + i], lg, tk[0:n, :], ALU.add))
            dve.wait_ge(S("ranks"), 1)
            cnt = psum[0:1, 3, 0:NE]
            do(v.tensor_scalar(cumf[:, 0, 1:], cnt, float(SLOT), 1.0, ALU.is_gt, ALU.add))
            for b in range(2, MAXB):
                do(v.scalar_tensor_tensor(out=cumf[:, (b - 1) % 2, 1:], in0=cnt, scalar=float(b * SLOT), in1=cumf[:, b % 2, 1:],
                                          op0=ALU.is_gt, op1=ALU.add))
            do(v.memset(cumf[:, 2, 0:1], 0.0))
            do(v.tensor_tensor_scan(cumf[:, 2, 1:], ones[0:1, 0:NE], cumf[:, (MAXB - 2) % 2, 1:], 0.0, ALU.mult, ALU.add))
            do(v.tensor_copy(cum[:, :], cumf[:, 2, :]))
            dve.sem_inc(S("cum_ready"), 1)
            for i, (t0, n) in enumerate(TILES):
                do(v.scalar_tensor_tensor(out=tk[0:n, :], in0=psum[0:n, 4, i * NE:(i + 1) * NE], scalar=1.0, in1=msk[0:n, i, :],
                                          op0=ALU.add, op1=ALU.mult))
                do(v.tensor_scalar(tab[0:n, :, i], tk[0:n, :], 1.0, None, ALU.subtract))
                dve.sem_inc(S("tab_ready"), 1)
            dve.wait_ge(S("gTp"), 1)
            v.tensor_copy(gT, psum[0:NE, 5, 0:T]).then_inc(S("gT_ready"), 1)
            for i, (t0, n) in enumerate(TILES):
                for hf in range(2):
                    dve.wait_ge(S("bias_mm"), 2 * i + hf + 1)
                    x = acc[0:n, i, hf * 512:(hf + 1) * 512]
                    v.tensor_tensor(x, x, psum[0:n, 6 + hf, :], ALU.add).then_inc(S("bias_added"), 1)
            dve.wait_ge(S("bias_added"), 6)

            def x_columns(g):
                dve.wait_ge(S("gathered"), g + 2)
                v.tensor_copy(flat(xeT), psum[:, XB, :]).then_inc(S("xe_ready"), 1)

            def add(g, k):
                i, hf = k // 2, k % 2
                n = TILES[i][1]
                dve.wait_ge(S("combined"), 6 * g + (k + 1))
                x = acc[0:n, i, hf * 512:(hf + 1) * 512]
                v.tensor_tensor(x, x, psum[0:n, CB + hf, :], ALU.add).then_inc(S("added"), 1)

            x_columns(0)
            with dve.Fori(0, NE) as e:
                first = dve.value_load(cum[0:1, bass.ds(e, 1)], min_val=0, max_val=NE * MAXB)
                end = dve.value_load(cum[0:1, bass.ds(e + 1, 1)], min_val=1, max_val=NE * MAXB)
                with dve.Fori(first, end) as g:
                    x_columns(g + 1)
                    bias = bg[:, bass.ds(e, 1), :, :].rearrange("p o g m -> p (o m) g")
                    for hf in range(2):
                        m4 = slice(4 * hf, 4 * hf + 4)
                        dve.wait_ge(S("turned"), 2 * g + (hf + 3))
                        v.tensor_tensor(hb[:, m4], cut(psum[:, DN + hf, :], 4, 2, SLOT),
                                        bias[:, m4, :, None].to_broadcast([P, 4, 2, SLOT]), ALU.add).then_inc(S("biased"), 1)
                        dve.wait_ge(S("biased"), 2 * g + (hf + 1))
                        v.tensor_scalar(hb[:, m4, 0, :], hb[:, m4, 0, :], LIMIT, None, ALU.min).then_inc(S("clamped"), 1)
                        v.tensor_scalar(hb[:, m4, 1, :], hb[:, m4, 1, :], LIMIT, -LIMIT, ALU.min, ALU.max).then_inc(S("up_clamped"), 1)
                    for hf in range(2):
                        m4 = slice(4 * hf, 4 * hf + 4)
                        add(g, hf)
                        dve.wait_ge(S("sg_ready"), 2 * g + (hf + 1))
                        v.tensor_tensor(sg[:, m4], hb[:, m4, 0, :], sg[:, m4], ALU.mult).then_inc(S("swished"), 1)
                        dve.wait_ge(S("swished"), 2 * g + (hf + 1))
                        dve.wait_ge(S("up_clamped"), 2 * g + (hf + 1))
                        v.scalar_tensor_tensor(out=hT[:, m4], in0=hb[:, m4, 1, :], scalar=1.0, in1=sg[:, m4],
                                               op0=ALU.add, op1=ALU.mult).then_inc(S("hT_ready"), 1)
                    for k in range(2, 6):
                        add(g, k)
                    dve.wait_ge(S("pt_done"), g + 2)
                    v.tensor_copy(pt, psum[:, PTB, 0:T]).then_inc(S("pt_ready"), 1)
            blocks = dve.value_load(cum[0:1, NE:NE + 1], min_val=1, max_val=NE * MAXB)
            for k in range(6):
                add(blocks, k)
            dve.wait_ge(S("added"), 6 * blocks + 8)
            dve.sem_inc(S("acc_ready"), 1)
            dve.wait_ge(S("nfb_landed"), 16)
            for i, (t0, n) in enumerate(TILES):
                inv = inverse_rms(i, n, 2)
                v.scalar_tensor_tensor(out=acc[0:n, i, :], in0=acc[0:n, i, :], scalar=inv, in1=nfb[0:n, :],
                                       op0=ALU.mult, op1=ALU.mult).then_inc(S("y_ready"), 1)


_INS = ["x_prompt", "x_sample", "state_s5_re", "state_s5_im", "state_ml_C", "state_ml_n", "state_ml_m",
        "norm_mix", "w_in", "b_ig", "b_fg", "s5_a_re", "s5_a_im", "s5_log_dt", "s5_b_re", "s5_b_im",
        "s5_c_re", "s5_c_im", "s5_d", "w_s5_glu", "ml_gn", "w_ml_out", "w_out", "norm_moe", "w_router",
        "b_router", "w_gate_up", "b_gate_up", "w_down", "b_down", "norm_final"]
_STATES = [(1, 1, S5G, S5P), (1, 1, S5G, S5P), (1, 1, H, HD, HD), (1, 1, H, HD), (1, 1, H)]
_OUTS = [(1, TP, D), (1, TS, D)] + _STATES + _STATES


def kernel(**inputs):
    import numpy as _np
    import concourse.bacc as _bacc
    from concourse import mybir as _mybir
    from concourse.bass_utils import run_bass_kernel_spmd as _run

    nc = _bacc.Bacc("TRN2", target_bir_lowering=False, num_devices=1)
    arrays, args = {}, {}
    for name in _INS + ["consts"]:
        x = shape_constants() if name == "consts" else _np.ascontiguousarray(inputs[name])
        arrays[f"in_{name}_dram"] = x
        args[name] = nc.dram_tensor(f"in_{name}_dram", x.shape, _mybir.dt.from_np(x.dtype), kind="ExternalInput").ap()
    outs = [nc.dram_tensor(f"out_{i}_dram", s, F32, kind="ExternalOutput").ap() for i, s in enumerate(_OUTS)]
    hybrid_stream_step(nc, args, outs)
    r = _run(nc, [arrays], core_ids=[0])
    return tuple(r.results[0][f"out_{i}_dram"] for i in range(len(_OUTS)))
```

```python
from contextlib import ExitStack

import numpy as np

import concourse.bass as bass
from concourse import mybir

P = 128
ALU = mybir.AluOpType
ACT = mybir.ActivationFunctionType
AX_X = mybir.AxisListType.X
F32 = mybir.dt.float32
BF16 = mybir.dt.bfloat16
I32 = mybir.dt.int32
U32 = mybir.dt.uint32

D = 1024
DK = D // P
TP, TS = 256, 64
T = TP + TS
TILES = [(0, 128), (128, 128), (256, 64)]
CH = 64
NC = T // CH
NCP = TP // CH
DS5, S5G, S5C, S5P = 512, 32, 16, 64
NJ = S5G * S5P // P
H, HD = 4, 128
NE, TOPK, FF = 32, 4, 1024
FK = FF // P
SLOT = 64
MAXB = -(-T // SLOT)
EPS = 1e-6
LIMIT, ALPHA = 7.0, 1.702
D_IN = DS5 + 4 * H * HD + 2 * H + 2 * D
GATE0 = DS5 + 4 * H * HD
TWO_PI = 6.283185307179586
PI2_A = 6.28125
PI2_B = float(np.float32(np.round((TWO_PI - PI2_A) * 2 ** 21) / 2 ** 21))
PI2_C = TWO_PI - PI2_A - PI2_B
PI_IN = 3.1415925
ROUND = 1.5 * 2 ** 23

C_ID, C_TRI, C_ONE, C_SLOT, C_EXP = 0, 128, 256, 384, 512
C_KEEP = 544
C_CAUSAL, C_PAR, C_HEAD, C_SEG = 544, 608, 610, 1122
C_ALL = C_SEG + T

CHUNK = 2048
RING = 16
GU_CHUNKS, DN_CHUNKS = DK, FK // 2
CHUNKS = GU_CHUNKS + DN_CHUNKS
TURN = 4
assert TURN * CHUNKS % RING == 0 and NE % TURN == 0


def shape_constants():
    c = np.zeros((P, C_ALL), np.float32)
    r = np.arange(P)
    c[:, C_ID:C_ID + P] = np.eye(P)
    c[:, C_TRI:C_TRI + P] = r[:, None] < r[None, :]
    c[:, C_ONE:C_ONE + P] = 1.0
    c[:, C_SLOT:C_SLOT + P] = (r % SLOT + 1)[None, :]
    c[:, C_EXP:C_EXP + NE] = np.arange(NE)[None, :]
    s = np.arange(CH)
    c[:CH, C_CAUSAL:C_CAUSAL + CH] = np.where(s[:, None] <= s[None, :], 0.0, -1e30)
    for par in range(2):
        c[:, C_PAR + par] = (r // S5C) % 2 == par
    for h in range(H):
        c[h, C_HEAD + h * P:C_HEAD + (h + 1) * P] = 1.0
    c[:H, C_SEG:C_SEG + T] = (np.arange(T) % CH != 0)[None, :]
    return c


def hybrid_stream_step(nc, a, out):
    with ExitStack() as ctx:
        def sb(name, shape, dt=F32):
            return ctx.enter_context(nc.sbuf_tensor(name, shape, dt))

        sems = {}

        def S(name):
            if name not in sems:
                sems[name] = ctx.enter_context(nc.semaphore(name))
            return sems[name]

        class Order:

            def __init__(self, eng, name):
                self.eng, self.sem, self.count = eng, S(name), 0

            def start(self, ins):
                self.count += 1
                ins.then_inc(self.sem, 1)

            def wait(self):
                self.eng.wait_ge(self.sem, self.count)

            def __call__(self, ins):
                self.start(ins)
                self.wait()

        FIRST = CHUNKS * CHUNK
        big = sb("big", [P, FIRST + 3 * DK * T + 4 * T])
        ring, after = big[:, 0:FIRST], big[:, FIRST:]
        m2 = sb("m2", [P, 12288])
        acc = sb("acc", [P, 3, D])
        uT = sb("uT", [P, 4, T])
        bg = sb("bg", [P, NE, 2, FK])
        cst = sb("cst", [P, C_KEEP])
        vc = sb("vc", [P, 16])
        st = sb("st", [P, 24])
        tab = sb("tab", [P, NE, 6])
        sm = sb("sm", [P, 640])
        rm = sb("rm", [H, T])
        cum = sb("cum", [1, NE + 1], I32)
        cumf = sb("cumf", [1, 4, NE + 1])
        psum = ctx.enter_context(nc.psum_tensor("psum", [P, 8, 512], F32))
        PJ = [psum[:, 0], psum[:, 1], psum[:, 4], psum[:, 5]]
        GU, DN, XB, PTB, CB = 0, 2, 4, 5, 6

        XT = (2, 6, 4)

        ident = cst[:, C_ID:C_ID + P]
        ones = cst[:, C_ONE:C_ONE + P]

        def flat(t):
            n = len(t.shape)
            if n == 2:
                return t[:, :]
            names = " ".join("abcde"[:n - 1])
            return t.rearrange(f"p {names} -> p ({names})")

        def cut(ap, *dims):
            names = "abcde"[:len(dims)]
            return ap.rearrange(f"p ({' '.join(names)}) -> p {' '.join(names)}", **dict(zip(names, dims)))

        gates = cut(after[:, 0:2 * DK * T], 2, DK, T)
        xnT = cut(after[:, 2 * DK * T:3 * DK * T], DK, T)
        oT = cut(after[:, 3 * DK * T:], 4, T)

        class Space:
            def __init__(self, buf, start=0, end=None):
                self.buf, self.at, self.end = buf, start, end or buf.shape[1]

            def take(self, *dims):
                n = int(np.prod(dims))
                self.at += n
                assert self.at <= self.end
                return cut(self.buf[:, self.at - n:self.at], *dims) if len(dims) > 1 else self.buf[:, self.at - n:self.at]

        r = Space(ring)
        ct = r.take(NJ, T)
        sn = r.take(NJ, T)
        btz = r.take(2, NJ, P)
        ctt = r.take(2, 4, P)
        WORK = r.at
        zz = r.take(2, 2, T)
        dtmp = r.take(2, T)
        ptmp = r.take(2, T)
        hh = r.take(2, 2, T)
        WORK_END = r.at
        qT, kT, vT = r.take(4, T), r.take(4, T), r.take(4, T)
        wg = r.take(DK, 36)
        cst2 = r.take(C_ALL - C_KEEP)
        w = Space(ring, WORK, WORK_END)
        bnat, bpad = w.take(2, NJ, S5C), w.take(2, NJ, 32)
        cnat, cpad = w.take(2, 4, S5P), w.take(2, 4, 2, S5P)
        w = Space(ring, WORK, WORK_END)
        num = w.take(H, HD + 1)[0:CH]
        hn = w.take(H, HD)[0:CH]
        vw = w.take(H, HD + 1)[0:CH]
        w = Space(ring)
        stage = [(w.take(H, HD), w.take(HD)[0:H]) for _ in range(2)]
        stage5 = w.take(4, P)[0:NJ]
        w = Space(flat(gates[:, :, :, :]))
        prm = w.take(20, P)[0:NJ]
        (A_RE, A_IM, H0R, H0I, DAI, RED, MAG, COS, SIN, FR, FI, X0, X1, X2, DEN, LDT) = range(16)
        btmp = w.take(4, P)
        vecs = w.take(P)[0:16]
        c0n = w.take(H, P)
        n0n = w.take(P)[0:H]
        gS, gM = gates[:, 0], gates[:, 1]

        wr = cut(m2[:, 0:3 * CHUNK], 3, CHUNK)
        w = Space(m2, 3 * CHUNK)
        xn = w.take(3, D)
        w = Space(m2, 3 * CHUNK)
        ttmp = [w.take(NJ // 2, P), w.take(NJ // 2, P)]
        btmp2 = w.take(4, NJ, S5C)
        w = Space(m2, 3 * CHUNK)
        kn = w.take(NC, H, HD)[0:CH]
        WT_AT = w.at
        wt = w.take(H, NC, CH)[0:CH]
        cn = w.take(2, H, HD + 1)
        cn0 = w.take(H, HD + 1)
        gtmp = [m2[:, m2.shape[1] - T:], m2[:, WT_AT:WT_AT + T]]
        vn = cut(flat(acc[:, :, :])[0:CH, 0:NC * H * (HD + 1)], NC, H, HD + 1)

        w = Space(m2, 0, 3 * CHUNK)
        gus = w.take(2 * 512)
        hb = w.take(FK, 2, SLOT)
        osb = w.take(2 * 512)
        xeT, sg, hT = w.take(DK, SLOT), w.take(FK, SLOT), w.take(FK, SLOT)
        pb = cut(w.take(96).bitcast(BF16), 3, SLOT)
        pw = w.take(3, P)
        pt = w.take(T)
        cur = w.take(6)
        w = Space(m2, 3 * CHUNK)
        parts = cut(w.take(3 * 3 * D // 2).bitcast(BF16), 3, 3, D)
        nmb = w.take(D)
        rest = cut(m2[:, CHUNK:CHUNK + 3 * D], 3, D)
        square2 = cut(m2[:, 0:3 * D], 3, D)
        bd3 = cut(w.take(D // 2).bitcast(BF16), 1, D)[0:3 * NE, 0]
        nfb = nmb
        sel = cut(flat(uT[:, :, :])[:, 0:NE * SLOT // 2].bitcast(BF16), NE, SLOT)[0:3 * NE]
        bdn = flat(oT[:, :, :])[0:3 * NE, 0:D]
        w = Space(flat(gates[:, :, :, :]), DK * T)
        xm01 = w.take(2, D)
        xm = [xm01[:, 0], xm01[:, 1], flat(gates[:, :, :, :])[:, 0:D]]
        brt = flat(oT[:, :, :])[:, D:D + NE]
        wrt = cut(flat(uT[:, :, :])[:, D:4 * T], DK, NE)

        w = Space(sm)
        pcol = w.take(7, NJ)
        M_FR, M_FI, M_MAG, M_COS, M_SIN, M_H0R, M_H0I = range(7)
        fin = w.take(4, NJ)
        wcol = w.take(3, NC, H)[0:CH]
        dec = w.take(H, NC)
        bns, mv = w.take(H, 6), w.take(H, 2)
        den = w.take(2 * H)
        bcol = w.take(2)
        top = [(w.take(NE), w.take(8), w.take(8).bitcast(U32), w.take(16)) for _ in TILES]
        msk = w.take(3, NE)
        tk = w.take(NE)
        (R_IG, R_LF, R_B, R_M, R_A, R_AL, R_WI, R_WE) = range(8)

        rows = [oT[0:H, k, :] for k in range(4)]
        rows += [flat(cn)[0:H, k * T:(k + 1) * T] for k in range(3)]
        rows.insert(R_M, rm[:, :])

        def by_chunk(k):
            return cut(rows[k], NC, CH)

        x_rows = [a["x_prompt"][0, 0:128, :], a["x_prompt"][0, 128:256, :], a["x_sample"][0, :, :]]
        y_rows = [out[0][0, 0:128, :], out[0][0, 128:256, :], out[1][0, :, :]]
        w_in = a["w_in"][0].rearrange("(k p) n -> p k n", p=P)
        w_glu = a["w_s5_glu"][0].rearrange("(k p) n -> p k n", p=P)
        w_ml = a["w_ml_out"][0].rearrange("(k p) n -> p k n", p=P)
        w_out = a["w_out"][0].rearrange("(k p) n -> p k n", p=P)

        groups = []
        for g in range(18):
            c = 256 * g if g < 10 else GATE0 + 2 * H + 256 * (g - 10)
            groups.append([(DK, 0, w_in[:, :, c:c + 256])])
        for g in range(4):
            groups.append([(4, 0, w_glu[:, :, 256 * g:256 * g + 256]),
                           (4, 256, w_glu[:, :, D + 256 * g:D + 256 * g + 256])])
        for g in range(2):
            groups.append([(4, 0, w_ml[:, :, 512 * g:512 * g + 512])])
        for g in range(4):
            groups.append([(DK, 0, w_out[:, :, 256 * g:256 * g + 256])])
        landed, total = [], [0, 0, 0]
        for g, dmas in enumerate(groups):
            total[g % 3] += 16 * len(dmas)
            landed.append(total[g % 3])
        G_IN, G_GLU, G_ML, G_OUT = 0, 18, 22, 24
        T_GLU, T_ML, T_OUT = 36, 52, 60
        T_FOUR = 36

        def bank(j):
            return PJ[j % 2] if j < T_FOUR else PJ[j % 4]

        SETUP_BIAS, SETUP_STATE, SETUP_C, SETUP_B = 1, 2, 3, 4

        S5_AT, ML_AT = 9, 27
        plan = {j: [] for j in range(T_ML)}
        for j, step in ((2, "s5_columns"), (3, "gate_rows"), (3, "tables"), (4, "biases"), (4, "state_in"), (5, "c_matrix"),
                        (6, "b_matrix"), (7, "row_factors"), (8, "row_columns")):
            plan[j].append((step, 0))
        for h in range(H):
            plan[9 + h].append(("decay_matrix", h))
        for j in range(NJ + 2):
            if j < NJ:
                plan[S5_AT + j].append(("s5_in", j))
            if j >= 2:
                plan[S5_AT + j].append(("s5_out", j - 2))
        for c in range(NC):
            plan[17 + c].append(("natural", c))
        for h in range(H):
            plan[22 + h].append(("scores", h))
        for c in range(NC):
            plan[ML_AT + 2 * c].append(("chunk", c))
            plan[ML_AT + 2 * c].append(("group_root", c))
            plan[ML_AT + 2 * c + (2 if c < NCP else 3)].append(("turn", c))
        plan[38] += [("states_out", 0)]
        plan[40] += [("states_out", 1), ("s5_out_states", 0)]
        for j in plan:
            plan[j].sort(key=lambda s: s[0] == "chunk")

        def by_tile(x):
            return x.rearrange("(j g) s -> j (g s)", g=2)

        block = ctx.enter_context(nc.Block())

        def slot(r, c):
            return (r * CHUNKS + c) % RING

        def loads(turn_, r, c):
            return turn_ * (TURN * CHUNKS // RING) + (r * CHUNKS + c) // RING + 1

        def expert_chunk(eng, turn_, r, c):
            e, k = turn_ * TURN + r, slot(r, c)
            dst = big[:, k * CHUNK:(k + 1) * CHUNK]
            if c < GU_CHUNKS:
                src = a["w_gate_up"][0, bass.ds(e, 1), c * P:(c + 1) * P, :].rearrange("a p n -> p (a n)")
            else:
                row = 2 * (c - GU_CHUNKS) * P
                src = a["w_down"][0, bass.ds(e, 1), row:row + 2 * P, :].rearrange("a (k p) n -> p (a k) n", p=P)
                dst = cut(dst, 2, D)
            eng.dma_start(dst, src).then_inc(S(f"w_landed{k}"), 16)

        @block.sync
        def _(sp):
            for i, (t0, n) in enumerate(TILES):
                sp.dma_start(acc[0:n, i, :], x_rows[i]).then_inc(S(f"x_landed{i}"), 16)
            sp.dma_start(cst[:, :], a["consts"][:, 0:C_KEEP]).then_inc(S("cst_landed"), 16)
            sp.dma_start(vecs[0:8, :], a["norm_mix"][0].rearrange("(k p) -> k p", p=P)).then_inc(S("vecs_landed"), 16)
            sp.dma_start(vecs[8:12, :], a["s5_d"][0].rearrange("(k p) -> k p", p=P)).then_inc(S("vecs_landed"), 16)
            sp.dma_start(vecs[12:16, :], a["ml_gn"][0].rearrange("(k p) -> k p", p=P)).then_inc(S("vecs_landed"), 16)
            for g, dmas in enumerate(groups):
                if g >= 3:
                    sp.wait_ge(S("group_used"), g - 2)
                for kk, c0, src in dmas:
                    dst = cut(wr[:, g % 3], kk, CHUNK // kk)[:, :, c0:c0 + src.shape[2]]
                    sp.dma_start(dst, src).then_inc(S(f"slot_landed{g % 3}"), 16)
                if g == 0:
                    for n, x in ((A_RE, a["s5_a_re"][0]), (A_IM, a["s5_a_im"][0]), (H0R, a["state_s5_re"][0, 0]), (H0I, a["state_s5_im"][0, 0])):
                        sp.dma_start(prm[:, n, :], by_tile(x)).then_inc(S("prm_landed"), 16)
                    sp.dma_start(prm[:, LDT, 0:2], a["s5_log_dt"][0].rearrange("(j g) -> j g", g=2)).then_inc(S("prm_landed"), 16)
                if g == 23:
                    sp.wait_ge(S("hT_read"), NC)
                    sp.wait_ge(S("cn_ready"), NC)
                    sp.wait_ge(S("co_read"), 4)
                    for i, (t0, n) in enumerate(TILES):
                        sp.dma_start(acc[0:n, i, :], x_rows[i]).then_inc(S("res_landed"), 16)
                    sp.dma_start(nmb, a["norm_moe"][0:1, :].to_broadcast([P, D])).then_inc(S("res_landed"), 16)
                if g == 25:
                    sp.wait_ge(S("pj_done"), T_OUT)
                    sp.dma_start(brt, a["b_router"][0:1, :].to_broadcast([P, NE])).then_inc(S("wrt_landed"), 16)
                    for q in range(3):
                        sp.dma_start(bdn[q * NE:(q + 1) * NE, :], a["b_down"][0]).then_inc(S("bdn_landed"), 16)
                if g == 23:
                    sp.wait_ge(S("pj_done"), T_ML)
                    sp.dma_start(wrt, a["w_router"][0].rearrange("(k p) e -> p k e", p=P)).then_inc(S("wrt_landed"), 16)
                if g >= 24:
                    sp.wait_ge(S("states_stored"), 160)
                    for c in range((g - 24) * 3, (g - 23) * 3):
                        expert_chunk(sp, 0, 0, c)
            sp.wait_ge(S("xm_ready"), 3)
            sp.dma_start(nfb, a["norm_final"].rearrange("(a d) -> a d", a=1).to_broadcast([P, D])).then_inc(S("nfb_landed"), 16)
            sp.wait_ge(S("parts_ready"), 1)
            sp.wait_ge(S("rest"), 3)
            sp.wait_ge(S("logits"), 3)
            for c in range(RING - CHUNKS):
                expert_chunk(sp, 0, 1, c)
            sp.wait_ge(S("cum_ready"), 1)

            def load_expert(turn_, r, peeled=False):
                e = turn_ * TURN + r
                if r != 1 or not peeled:
                    before = sp.value_load(cum[0:1, bass.ds(e - 1, 1)], min_val=0, max_val=NE * MAXB)
                    for c in range(RING - CHUNKS):
                        sp.wait_ge(S("chunks_used"), before * CHUNKS + (c + 2 * CHUNKS - RING + 1))
                        expert_chunk(sp, turn_, r, c)
                before = sp.value_load(cum[0:1, bass.ds(e, 1)], min_val=1, max_val=NE * MAXB)
                for c in range(RING - CHUNKS, CHUNKS):
                    sp.wait_ge(S("chunks_used"), before * CHUNKS + (c + CHUNKS - RING + 1))
                    expert_chunk(sp, turn_, r, c)

            for r in range(1, TURN):
                load_expert(0, r, peeled=True)
            with sp.Fori(1, NE // TURN) as turn_:
                for r in range(TURN):
                    load_expert(turn_, r)
            for i, (t0, n) in enumerate(TILES):
                sp.wait_ge(S("y_ready"), i + 1)
                sp.dma_start(y_rows[i], acc[0:n, i, :]).then_inc(S("y_stored"), 16)
            sp.wait_ge(S("y_stored"), 48)

        @block.tensor
        def _(pe):
            def turn(dst, src, n):
                return pe.transpose(dst, src, ident[0:n, 0:n])

            def head(h, n):
                c = C_HEAD - C_KEEP + h * P
                return cst2[0:H, c:c + n]

            def last_read(j):
                return j // 2 if j < T_FOUR + 2 else j // 2 - 1

            def project(j, g, kk, rhs, col):
                pe.wait_ge(S(f"slot_landed{g % 3}"), landed[g])
                if j >= 2:
                    pe.wait_ge(S(f"pj_free{j % 2}"), last_read(j))
                w = cut(wr[:, g % 3], kk, CHUNK // kk)
                for k in range(kk):
                    mm = pe.matmul(bank(j)[:, 0:T], w[:, k, col:col + P], rhs[:, k, :], start=(k == 0), stop=(k == kk - 1))
                mm.then_inc(S("pj_done"), 1)

            def group_used(j):
                pe.wait_ge(S("pj_done"), j + 1)
                pe.sem_inc(S("group_used"), 1)

            def s5_columns(_):
                pe.wait_ge(S("prm_ready"), 1)
                for n, k in enumerate((FR, FI, MAG, COS, SIN, H0R, H0I)):
                    mm = turn(psum[:, 2, n * NJ:(n + 1) * NJ], prm[:, k, :], NJ)
                mm.then_inc(S("prmT"), 1)

            def gate_rows(_):
                pe.wait_ge(S("wg_landed"), 32)
                for k in range(DK):
                    mm = pe.matmul(psum[0:36, 5, 0:T], wg[:, k, :], xnT[:, k, :], start=(k == 0), stop=(k == DK - 1))
                mm.then_inc(S("gate_mm"), 1)

            def biases(_):
                pe.wait_ge(S("btmp_landed"), 16)
                for q in range(4):
                    mm = turn(psum[:, 3, q * P:(q + 1) * P], btmp[:, q, :], P)
                mm.then_inc(S("setup_turned"), 1)

            def state_in(_):
                pe.wait_ge(S("c0_landed"), 32)
                for h in range(H):
                    turn(psum[:, 6, h * P:(h + 1) * P], c0n[:, h, :], P)
                turn(psum[:, 7, 0:H], n0n, H).then_inc(S("setup_turned"), 1)

            def c_matrix(_):
                pe.wait_ge(S("cpad_ready"), 1)
                pe.wait_ge(S("setup_read"), SETUP_STATE)
                for k in range(2):
                    for q in range(4):
                        mm = turn(psum[:, 6 + k, q * P:(q + 1) * P], flat(cpad[:, k, q]), P)
                mm.then_inc(S("setup_turned"), 1)

            def b_matrix(_):
                pe.wait_ge(S("bpad_ready"), 1)
                pe.wait_ge(S("setup_read"), SETUP_C)
                for k in range(2):
                    for q in range(4):
                        mm = turn(psum[:, 6 + k, q * P:(q + 1) * P], flat(bpad[:, k, 4 * q:4 * q + 4]), P)
                mm.then_inc(S("setup_turned"), 1)

            def row_columns(_):
                pe.wait_ge(S("rows_ready"), 1)
                pe.wait_ge(S("pcol_ready"), 1)
                pe.wait_ge(S("setup_read"), SETUP_BIAS)
                for n, k in enumerate((R_WI, R_WE, R_M)):
                    for c in range(NC):
                        o = (n * NC + c) * H
                        turn(psum[0:CH, 2, o:o + H], by_chunk(k)[:, c, :], H)
                for h in range(H):
                    mm = pe.matmul(psum[:, 3, h * NC:(h + 1) * NC], head(h, P), by_chunk(R_WI)[:, :, CH - 1], start=True, stop=True)
                mm.then_inc(S("cols_mm"), 1)

            def decay_matrix(h):
                if h == 0:
                    pe.wait_ge(S("setup_read"), SETUP_B)
                if h >= 2:
                    pe.wait_ge(S("dm_read"), h - 1)
                b = 6 + h % 2
                pe.matmul(psum[0:CH, b, 0:T], head(h, CH), rows[R_AL], start=True, stop=False, skip_group_check=True)
                for c in range(NC):
                    mm = pe.matmul(psum[0:CH, b, c * CH:(c + 1) * CH], by_chunk(R_A)[:, c, :], head(h, CH),
                                   start=False, stop=(c == NC - 1), skip_group_check=True)
                mm.then_inc(S("dm_done"), 1)

            def s5_in(j):
                if j == 0:
                    pe.wait_ge(S("cols_ready"), 1)
                    pe.wait_ge(S("u_ready"), 1)
                else:
                    pe.wait_ge(S("bu_read"), j)
                for k in range(2):
                    mm = pe.matmul(psum[:, 2 + k, 0:T], btz[:, k, j, :], uT[:, j // 4, :], start=True, stop=True)
                mm.then_inc(S("bu_done"), 1)

            def s5_out(j):
                q, t = j % 4, j // 4
                pe.wait_ge(S("h_ready"), j + 1)
                if q == 0 and t > 0:
                    pe.wait_ge(S("y_read"), t)
                for k in range(2):
                    mm = pe.matmul(psum[32 * q:32 * q + 32, 4, 0:T], ctt[:, k, t, 32 * q:32 * q + 32], hh[:, j % 2, k, :],
                                   start=(k == 0), stop=(k == 1))
                mm.then_inc(S("y_done"), 1)

            def natural(c):
                for n, src in enumerate((kT, vT)):
                    i = 2 * c + n
                    if i == 0:
                        pe.wait_ge(S("qkv_ready"), 1)
                        pe.wait_ge(S("dm_read"), 4)
                    if i >= 2:
                        pe.wait_ge(S("nat_read"), i - 1)
                    for h in range(H):
                        mm = turn(psum[0:CH, 6 + i % 2, h * P:(h + 1) * P], src[:, h, c * CH:(c + 1) * CH], P)
                    mm.then_inc(S("nat_done"), 1)

            def scores(h):
                if h == 0:
                    pe.wait_ge(S("nat_read"), 2 * NC)
                if h >= 2:
                    pe.wait_ge(S("st_ready"), h - 1)
                for c in range(NC):
                    mm = pe.matmul(psum[0:CH, 6 + h % 2, c * CH:(c + 1) * CH], kT[:, h, c * CH:(c + 1) * CH],
                                   qT[:, h, c * CH:(c + 1) * CH], start=True, stop=True)
                mm.then_inc(S("sc_done"), 1)

            def two(b, h, n):
                return psum[0:n, b + h // 2, (h % 2) * (HD + 1):(h % 2 + 1) * (HD + 1)]

            def chunk(c):
                if c > 0:
                    if c < NCP:
                        pe.wait_ge(S("cn_ready"), c)
                    else:
                        pe.wait_ge(S("num_read"), c)
                    state = cn[:, c % 2] if c < NCP else cn0
                    for h in range(H):
                        mm = pe.matmul(two(4, h, CH), qT[:, h, c * CH:(c + 1) * CH], state[:, h, :], start=True, stop=True)
                    mm.then_inc(S("b_done"), 1)
                pe.wait_ge(S("vw_ready"), c + 1)
                if c == 0:
                    pe.wait_ge(S("st_ready"), H)
                if c == NCP:
                    pe.wait_ge(S("cn_ready"), c)
                for h in range(H):
                    mm = pe.matmul(two(6, h, P), kn[:, c, h, :], vw[:, h, :], start=True, stop=True)
                mm.then_inc(S("u_done"), 1)
                if c == 0:
                    pe.wait_ge(S("y_read"), 4)
                    pe.wait_ge(S("bu_read"), NJ)
                else:
                    pe.wait_ge(S("hT_read"), c)
                for h in range(H):
                    mm = pe.matmul(two(2, h, CH), wt[:, h, c, :], vn[:, c, h, :], start=True, stop=True)
                mm.then_inc(S("a_done"), 1)

            def turn_chunk(c):
                pe.wait_ge(S("hn_ready"), c + 1)
                for h in range(H):
                    mm = turn(psum[:, 2, h * CH:(h + 1) * CH], hn[:, h, :], CH)
                mm.then_inc(S("hT_done"), 1)

            def states_out(s):
                pe.wait_ge(S("cn_ready"), NC)
                if s == 1:
                    pe.wait_ge(S("co_read"), 2)
                for h in range(H):
                    turn(psum[:, 6, h * P:(h + 1) * P], cn[:, s, h, 0:HD], P)
                turn(psum[0:H, 7, 0:P], cn[:, s, :, HD], P).then_inc(S("co_done"), 1)

            def s5_out_states(_):
                pe.wait_ge(S("fin_ready"), 2 * NJ)
                pe.wait_ge(S("hT_read"), NC)
                for n in range(4):
                    mm = turn(psum[0:NJ, 2, n * P:(n + 1) * P], fin[:, n, :], P)
                mm.then_inc(S("finT"), 1)

            steps = dict(s5_columns=s5_columns, gate_rows=gate_rows, biases=biases, state_in=state_in,
                         c_matrix=c_matrix, b_matrix=b_matrix, row_columns=row_columns, decay_matrix=decay_matrix,
                         s5_in=s5_in, s5_out=s5_out, natural=natural, scores=scores, chunk=chunk, turn=turn_chunk,
                         states_out=states_out, s5_out_states=s5_out_states)

            pe.wait_ge(S("cst_landed"), 16)
            pe.wait_ge(S("vecs_landed"), 48)
            turn(psum[:, 0, 0:16], vecs, 16).then_inc(S("vcT"), 1)
            for i, (t0, n) in enumerate(TILES):
                pe.wait_ge(S("xn_ready"), i + 1)
                for k in range(DK):
                    mm = turn(psum[:, 2 + 2 * i + k // 4, (k % 4) * P:(k % 4) * P + n], xn[0:n, i, k * P:(k + 1) * P], n)
                mm.then_inc(S("xT"), 1)
            pe.wait_ge(S("xnT_ready"), 3)
            pe.wait_ge(S("vc_ready"), 1)
            for j in range(T_GLU):
                project(j, j // 2, DK, xnT, (j % 2) * P)
                if j % 2 == 1:
                    group_used(j)
                if j == 2:
                    pe.wait_ge(S("cst2_landed"), 16)
                for step, i in plan[j]:
                    if step in steps:
                        steps[step](i)
            pe.wait_ge(S("gelu_ready"), 4)
            for i in range(16):
                j = T_GLU + i
                if j == T_FOUR + 2:
                    pe.wait_ge(S("num_read"), NC)
                project(j, G_GLU + i // 4, 4, uT, (i % 4 // 2) * P + (i % 2) * 256)
                if i % 4 == 3:
                    group_used(j)
                for step, n in plan[j]:
                    if step in steps:
                        steps[step](n)
            pe.wait_ge(S("hT_read"), NC)
            for i in range(8):
                j = T_ML + i
                project(j, G_ML + i // 4, 4, oT, (i % 4) * P)
                if i % 4 == 3:
                    group_used(j)
            pe.wait_ge(S("mix_ready"), 8)
            j = T_OUT
            for g in range(G_OUT, G_OUT + 4):
                pe.wait_ge(S(f"slot_landed{g % 3}"), landed[g])
                for i, (t0, n) in enumerate(TILES):
                    pe.wait_ge(S(f"pj_free{j % 2}"), last_read(j))
                    for k in range(DK):
                        mm = pe.matmul(bank(j)[0:n, 0:256], gS[:, k, t0:t0 + n], cut(wr[:, g % 3], DK, 256)[:, k, :],
                                       start=(k == 0), stop=(k == DK - 1))
                    mm.then_inc(S("pj_done"), 1)
                    j += 1
                group_used(j - 1)

            def rows_turned(i):
                t0, n = TILES[i]
                pe.wait_ge(S("xm_ready"), i + 1)
                for k in range(DK):
                    mm = turn(psum[:, XT[i] + k // 4, (k % 4) * P:(k % 4) * P + n], xm[i][0:n, k * P:(k + 1) * P], n)
                mm.then_inc(S("xmT"), 1)

            def logits(i):
                t0, n = TILES[i]
                pe.wait_ge(S("xmT_ready"), i + 1)
                for k in range(DK):
                    mm = pe.matmul(psum[0:n, i, 0:NE], xnT[:, k, t0:t0 + n], wrt[:, k, :],
                                   start=(k == 0), stop=(k == DK - 1))
                mm.then_inc(S("logits"), 1)

            rows_turned(0)
            rows_turned(1)
            pe.wait_ge(S("wrt_landed"), 32)
            logits(0)
            rows_turned(2)
            logits(1)
            logits(2)
            for i, (t0, n) in enumerate(TILES):
                pe.wait_ge(S("mask_ready"), i + 1)
                for b in range(i + 1):
                    nb = TILES[b][1]
                    before = cst[0:nb, C_TRI:C_TRI + n] if b == i else ones[0:nb, 0:n]
                    pe.matmul(psum[0:n, 4, i * NE:(i + 1) * NE], before, msk[0:nb, b, :], start=(b == 0), stop=(b == i))
            for b in range(3):
                nb = TILES[b][1]
                mm = pe.matmul(psum[0:1, 3, 0:NE], ones[0:nb, 0:1], msk[0:nb, b, :], start=(b == 0), stop=(b == 2))
            mm.then_inc(S("ranks"), 1)
            def gather(g):
                pe.wait_ge(S("p_ready"), g + 1)
                for k in range(DK):
                    for i in range(3):
                        for q in range(3):
                            mm = pe.matmul(psum[:, XB, k * SLOT:(k + 1) * SLOT], parts[:, q, i, k * P:(k + 1) * P], pb[:, i, :],
                                           start=(i == 0 and q == 0), stop=(i == 2 and q == 2))
                mm.then_inc(S("gathered"), 1)

            def combine(g, k):
                i, hf = k // 2, k % 2
                t0, n = TILES[i]
                if k == 0:
                    pe.wait_ge(S("osb_ready"), 2 * g + 2)
                    pe.wait_ge(S("pt_ready"), g + 1)
                pe.wait_ge(S("added"), 6 * g + k + 1)
                pe.matmul(psum[0:n, CB + hf, :], pt[:, t0:t0 + n], osb[:, hf * 512:(hf + 1) * 512],
                          start=True, stop=True).then_inc(S("combined"), 1)

            pe.wait_ge(S("sel_ready"), 3)
            pe.wait_ge(S("parts_ready"), 4)
            gather(0)
            pe.wait_ge(S("cum_ready"), 1)
            def expert(turn_, r):
                e = turn_ * TURN + r
                first = pe.value_load(cum[0:1, bass.ds(e, 1)], min_val=0, max_val=NE * MAXB)
                end = pe.value_load(cum[0:1, bass.ds(e + 1, 1)], min_val=1, max_val=NE * MAXB)
                with pe.Fori(first, end) as g:
                    pe.wait_ge(S("xe_ready"), g + 1)
                    pe.wait_ge(S("gus_ready"), 2 * g + 2)
                    for c in range(GU_CHUNKS):
                        pe.wait_ge(S(f"w_landed{slot(r, c)}"), 16 * loads(turn_, r, c))
                        for hf in range(2):
                            for gu in range(2):
                                base = slot(r, c) * CHUNK + gu * FF + hf * 512
                                mm = pe.matmul(psum[64 * gu:64 * gu + 64, GU + hf, :], xeT[:, c, :], big[:, base:base + 512],
                                               start=(c == 0), stop=(c == GU_CHUNKS - 1))
                        mm.then_inc(S("chunks_used"), 1)
                        if 1 <= c <= 4:
                            combine(g, c - 1)
                    combine(g, 4)
                    combine(g, 5)
                    pe.wait_ge(S("pw_ready"), g + 1)
                    for i, (t0, n) in enumerate(TILES):
                        mm = turn(psum[:, PTB, t0:t0 + n], pw[0:n, i, :], n)
                    mm.then_inc(S("pt_done"), 1)
                    pe.wait_ge(S("gus_ready"), 2 * g + 4)
                    pe.wait_ge(S("osb_ready"), 2 * g + 2)
                    for m in range(FK):
                        mm = turn(psum[:, DN + m // 4, (m % 4) * P:(m % 4 + 1) * P], gus[:, m * P:(m + 1) * P], P)
                        if m % 4 == 3:
                            mm.then_inc(S("turned"), 1)
                    gather(g + 1)
                    pe.wait_ge(S("biased"), 2 * g + 2)
                    for hf in range(2):
                        pe.matmul(psum[0:SLOT, DN + hf, :], sel[:, bass.ds(e, 1), :].rearrange("p o s -> p (o s)"),
                                  bd3[:, hf * 512:(hf + 1) * 512], start=True, stop=False, skip_group_check=True)
                    pe.wait_ge(S("hT_ready"), 2 * g + 2)
                    for c in range(DN_CHUNKS):
                        k_down = slot(r, GU_CHUNKS + c)
                        pe.wait_ge(S(f"w_landed{k_down}"), 16 * loads(turn_, r, GU_CHUNKS + c))
                        for hf in range(2):
                            for k in range(2):
                                base = k_down * CHUNK + k * D + hf * 512
                                mm = pe.matmul(psum[64 * k:64 * k + 64, DN + hf, :], hT[:, 2 * c + k, :], big[:, base:base + 512],
                                               start=(c == 0 and k == 1), stop=(c == DN_CHUNKS - 1), skip_group_check=True)
                        mm.then_inc(S("chunks_used"), 1)
            with pe.Fori(0, NE // TURN) as turn_:
                for r in range(TURN):
                    expert(turn_, r)
            blocks = pe.value_load(cum[0:1, NE:NE + 1], min_val=1, max_val=NE * MAXB)
            for k in range(6):
                combine(blocks, k)

        @block.scalar
        def _(act):
            do = Order(act, "act_order")

            for i, (t0, n) in enumerate(TILES):
                act.wait_ge(S(f"x_landed{i}"), 16)
                nc.scalar.activation(xn[0:n, i, :], acc[0:n, i, :], ACT.Square, accum_out=st[0:n, i:i + 1]).then_inc(S("ss"), 1)
                act.wait_ge(S("ms"), i + 1)
                nc.scalar.activation(st[0:n, 6 + i:7 + i], st[0:n, 3 + i:4 + i], ACT.Sqrt).then_inc(S("rms"), 1)
            act.wait_ge(S("wg_zero"), 1)
            act.dma_start(wg[:, :, 0:H], w_in[:, :, GATE0:GATE0 + H]).then_inc(S("wg_landed"), 16)
            act.dma_start(wg[:, :, 32:32 + H], w_in[:, :, GATE0 + H:GATE0 + 2 * H]).then_inc(S("wg_landed"), 16)
            act.dma_start(cst2, a["consts"][:, C_KEEP:C_ALL]).then_inc(S("cst2_landed"), 16)
            for k, x in enumerate((a["s5_c_re"][0], a["s5_c_im"][0])):
                act.dma_start(cnat[:, k], x.rearrange("g c s -> (g c) s").rearrange("(q r) s -> r q s", r=P)).then_inc(S("cnat_landed"), 16)
            for k, x in enumerate((a["s5_b_re"][0], a["s5_b_im"][0])):
                act.dma_start(bnat[:, k], x.rearrange("g s c -> (g s) c").rearrange("(j r) c -> r j c", r=P)).then_inc(S("bnat_landed"), 16)
            act.dma_start(bcol[0:H, 0:1], a["b_ig"][0].rearrange("(h o) -> h o", o=1)).then_inc(S("bcol_landed"), 16)
            act.dma_start(bcol[32:32 + H, 0:1], a["b_fg"][0].rearrange("(h o) -> h o", o=1)).then_inc(S("bcol_landed"), 16)
            act.dma_start(bcol[0:H, 1:2], a["state_ml_m"][0, 0].rearrange("(h o) -> h o", o=1)).then_inc(S("bcol_landed"), 16)
            act.dma_start(btmp, a["b_gate_up"][0].rearrange("e (m p) -> (e m) p", p=P).rearrange("(q r) p -> r q p", r=P)).then_inc(S("btmp_landed"), 16)
            act.dma_start(c0n, a["state_ml_C"][0, 0].rearrange("h v k -> v h k")).then_inc(S("c0_landed"), 16)
            act.dma_start(n0n, a["state_ml_n"][0, 0]).then_inc(S("c0_landed"), 16)
            act.wait_ge(S("prm_landed"), 80)
            nc.scalar.activation(prm[:, LDT, 2:4], prm[:, LDT, 0:2], ACT.Exp).then_inc(S("dt_ready"), 1)
            act.wait_ge(S("dar"), 1)
            nc.scalar.activation(prm[:, MAG, :], prm[:, X0, :], ACT.Exp).then_inc(S("sincos"), 1)
            act.wait_ge(S("reduced"), 1)
            nc.scalar.activation(prm[:, SIN, :], prm[:, RED, :], ACT.Sin).then_inc(S("sincos"), 1)
            nc.scalar.activation(prm[:, COS, :], prm[:, X2, :], ACT.Sin).then_inc(S("sincos"), 1)

            def evac(j, dst, func=ACT.Copy, scale=1.0):
                act.wait_ge(S("pj_done"), j + 1)
                nc.scalar.activation(dst, bank(j)[:, 0:T], func, scale=scale).then_inc(S(f"pj_free{j % 2}"), 1)

            def publish(j, name):
                act.wait_ge(S("pj_free0"), j // 2 + 1)
                act.wait_ge(S("pj_free1"), (j + 1) // 2)
                act.sem_inc(S(name), 1)

            def gate_rows(_):
                act.wait_ge(S("gate_mm"), 1)
                act.wait_ge(S("bcol_landed"), 48)
                do(nc.scalar.activation(rows[R_IG], psum[0:H, 5, 0:T], ACT.Identity, bias=bcol[0:H, 0:1]))
                do(nc.scalar.activation(rows[R_LF], psum[32:32 + H, 5, 0:T], ACT.Identity, bias=bcol[32:32 + H, 0:1]))
                act.sem_inc(S("gate_rows"), 1)
                act.wait_ge(S("fabs"), 1)
                do(nc.scalar.activation(rows[R_A], rows[R_B], ACT.Exp, scale=-1.0))
                nc.scalar.activation(rows[R_AL], rows[R_A], ACT.Ln, bias=1.0).then_inc(S("softplus"), 1)

            def biases(_):
                act.wait_ge(S("setup_turned"), SETUP_BIAS)
                nc.scalar.copy(flat(bg[:, :, :, :]), psum[:, 3, :]).then_inc(S("setup_read"), 1)

            def state_in(_):
                act.wait_ge(S("setup_turned"), SETUP_STATE)
                do(nc.scalar.copy(cn0[:, :, 0:HD], cut(psum[:, 6, :], H, HD)))
                nc.scalar.copy(cn0[:, :, HD], psum[:, 7, 0:H]).then_inc(S("setup_read"), 1)

            def c_matrix(_):
                act.wait_ge(S("setup_turned"), SETUP_C)
                do(nc.scalar.copy(flat(ctt[:, 0]), psum[:, 6, :]))
                nc.scalar.mul(flat(ctt[:, 1]), psum[:, 7, :], -1.0).then_inc(S("setup_read"), 1)

            def b_matrix(_):
                act.wait_ge(S("setup_turned"), SETUP_B)
                act.wait_ge(S("btz_zero"), 1)
                for k in range(2):
                    for q in range(4):
                        s = slice(32 * q, 32 * q + 32)
                        do(nc.scalar.copy(btz[s, k, q:NJ:4, :], cut(psum[s, 6 + k, :], 4, P)))
                act.sem_inc(S("setup_read"), 1)

            def row_factors(_):
                act.wait_ge(S("wexp"), 1)
                do(nc.scalar.activation(rows[R_WI], rows[R_WI], ACT.Exp))
                nc.scalar.activation(rows[R_WE], rows[R_WE], ACT.Exp).then_inc(S("rows_ready"), 1)

            def row_columns(_):
                act.wait_ge(S("cols_mm"), 1)
                do(nc.scalar.copy(wcol[:, 0:2], cut(psum[0:CH, 2, 0:2 * NC * H], 2, NC, H)))
                do(nc.scalar.activation(wcol[:, 2], cut(psum[0:CH, 2, 2 * NC * H:3 * NC * H], NC, H), ACT.Exp, scale=-1.0))
                nc.scalar.copy(flat(dec), psum[:, 3, 0:H * NC]).then_inc(S("cols_ready"), 1)

            def decay_matrix(h):
                act.wait_ge(S("dm_read"), h + 1)
                nc.scalar.activation(wt[:, h], wt[:, h], ACT.Exp).then_inc(S("wt_ready"), 1)

            def natural(c):
                for i in (2 * c, 2 * c + 1):
                    act.wait_ge(S("nat_done"), i + 1)
                    if i == 1:
                        act.wait_ge(S("vn_ones"), 1)
                    dst = kn[:, c] if i % 2 == 0 else vn[:, c, :, 0:HD]
                    nc.scalar.copy(dst, cut(psum[0:CH, 6 + i % 2, :], H, HD)).then_inc(S("nat_read"), 1)

            def group_root(c):
                act.wait_ge(S("var_ready"), c + 1)
                nc.scalar.activation(den[0:CH, H:2 * H], den[0:CH, 0:H], ACT.Sqrt).then_inc(S("std_ready"), 1)

            def states_out(s):
                act.wait_ge(S("co_done"), s + 1)
                nc.scalar.copy(flat(stage[s][0]), psum[:, 6, :]).then_inc(S("co_read"), 1)
                nc.scalar.copy(stage[s][1], psum[0:H, 7, 0:P]).then_inc(S("co_read"), 1)
                act.wait_ge(S("co_read"), 2 * s + 2)
                o = 4 + 5 * s
                act.dma_start(out[o][0, 0].rearrange("h v k -> v h k"), stage[s][0]).then_inc(S("states_stored"), 16)
                act.dma_start(out[o + 1][0, 0], stage[s][1]).then_inc(S("states_stored"), 16)
                last = (TP if s == 0 else T) - 1
                act.dma_start(out[o + 2][0, 0].rearrange("(h o) -> h o", o=1), rows[R_M][:, last:last + 1]).then_inc(S("states_stored"), 16)

            def s5_out_states(_):
                act.wait_ge(S("finT"), 1)
                do(nc.scalar.copy(stage5, cut(psum[0:NJ, 2, :], 4, P)))
                for n, o in enumerate((2, 3, 7, 8)):
                    act.dma_start(by_tile(out[o][0, 0]), stage5[:, n, :]).then_inc(S("states_stored"), 16)

            steps = dict(gate_rows=gate_rows, biases=biases, state_in=state_in, c_matrix=c_matrix, b_matrix=b_matrix,
                         row_factors=row_factors, row_columns=row_columns, decay_matrix=decay_matrix, natural=natural,
                         group_root=group_root, states_out=states_out, s5_out_states=s5_out_states)

            for j in range(T_GLU):
                if j < 4:
                    evac(j, uT[:, j, :])
                elif j < 8:
                    evac(j, qT[:, j - 4, :], scale=HD ** -0.5)
                elif j < 12:
                    evac(j, kT[:, j - 8, :])
                elif j < 16:
                    evac(j, vT[:, j - 12, :])
                elif j < 20:
                    if j == 16:
                        act.wait_ge(S("dm_done"), H)
                    evac(j, oT[:, j - 16, :], ACT.Sigmoid)
                elif j < 28:
                    evac(j, gS[:, j - 20, :], ACT.Sigmoid)
                else:
                    evac(j, gM[:, j - 28, :], ACT.Sigmoid)
                if j == 3:
                    publish(j, "u_ready")
                if j == 15:
                    publish(j, "qkv_ready")
                if j == 35:
                    publish(j, "gates_ready")
                if j == 30:
                    for q in range(4):
                        act.wait_ge(S("y_read"), q + 1)
                        nc.scalar.activation(uT[:, q, :], uT[:, q, :], ACT.Gelu_apprx_tanh).then_inc(S("gelu_ready"), 1)
                for step, n in plan[j]:
                    if step in steps:
                        steps[step](n)
            for i in range(16):
                j = T_GLU + i
                if i % 2 == 1:
                    if i == 3:
                        act.wait_ge(S("a_done"), NC)
                    if i > 3:
                        act.wait_ge(S("glu_done"), i // 2 - 1)
                    evac(j, gtmp[i // 2 % 2], ACT.Sigmoid)
                for step, n in plan[j]:
                    if step in steps:
                        steps[step](n)

            act.wait_ge(S("mix_ready"), 8)
            for q in range(3):
                r32 = slice(q * NE, (q + 1) * NE)
                nc.scalar.copy(sel[r32], ident[r32, r32][:, :, None].to_broadcast([NE, NE, SLOT])).then_inc(S("sel_ready"), 1)

            def middle(i, n):
                act.wait_ge(S("rest"), i + 1)
                nc.scalar.copy(parts[0:n, 1, i, :], rest[0:n, i, :]).then_inc(S("mid_ready"), 1)

            act.wait_ge(S("zeros_set"), 1)

            def root_table():
                do(nc.scalar.activation(st[0:1, 12:13], ones[0:1, 0:1], ACT.Sqrt))

            root_table()

            def root(i):
                n = TILES[i][1]
                act.wait_ge(S("x1_ready"), i + 1)
                nc.scalar.activation(rest[0:n, i, :], acc[0:n, i, :], ACT.Square, accum_out=st[0:n, i:i + 1]).then_inc(S("ss"), 1)
                act.wait_ge(S("ms"), 4 + i)
                nc.scalar.activation(st[0:n, 6 + i:7 + i], st[0:n, 3 + i:4 + i], ACT.Sqrt).then_inc(S("rms"), 1)

            root(0)
            for i, (t0, n) in enumerate(TILES):
                if i == 1:
                    root(1)
                    root(2)
                act.wait_ge(S("xm_ready"), i + 1)
                nc.scalar.copy(parts[0:n, 0, i, :], xm[i][0:n, :]).then_inc(S("hi_ready"), 1)
                if i > 0:
                    middle(i - 1, P)
            middle(2, TS)
            for i, (t0, n) in enumerate(TILES):
                act.wait_ge(S("top_ready"), i + 1)
                _, t8, _, f8 = (x[0:n] for x in top[i])
                nc.scalar.activation(f8[:, 4:8], t8[:, 0:4], ACT.Exp, bias=f8[:, 8:9], accum_out=f8[:, 9:10]).then_inc(S("top_exp"), 1)
            act.wait_ge(S("cum_ready"), 1)
            with act.Fori(0, NE) as e:
                first = act.value_load(cum[0:1, bass.ds(e, 1)], min_val=0, max_val=NE * MAXB)
                end = act.value_load(cum[0:1, bass.ds(e + 1, 1)], min_val=1, max_val=NE * MAXB)
                with act.Fori(first, end) as g:
                    act.wait_ge(S("chunks_used"), CHUNKS * g + (CHUNKS + GU_CHUNKS))
                    act.wait_ge(S("turned"), 2 * g + 2)
                    for hf in range(2):
                        nc.scalar.copy(gus[:, hf * 512:(hf + 1) * 512], psum[:, GU + hf, :]).then_inc(S("gus_ready"), 1)
                    for hf in range(2):
                        act.wait_ge(S("clamped"), 2 * g + hf + 1)
                        nc.scalar.activation(sg[:, 4 * hf:4 * hf + 4, :], hb[:, 4 * hf:4 * hf + 4, 0, :], ACT.Sigmoid,
                                             scale=ALPHA).then_inc(S("sg_ready"), 1)
                    act.wait_ge(S("chunks_used"), CHUNKS * g + 2 * CHUNKS)
                    act.wait_ge(S("combined"), 6 * g + 6)
                    for hf in range(2):
                        nc.scalar.copy(osb[:, hf * 512:(hf + 1) * 512], psum[:, DN + hf, :]).then_inc(S("osb_ready"), 1)
            root_table()
            for i, (t0, n) in enumerate(TILES):
                act.wait_ge(S("acc_ready"), i + 1)
                nc.scalar.activation(square2[0:n, i, :], acc[0:n, i, :], ACT.Square, accum_out=st[0:n, i:i + 1]).then_inc(S("ss"), 1)
                act.wait_ge(S("ms"), 7 + i)
                nc.scalar.activation(st[0:n, 6 + i:7 + i], st[0:n, 3 + i:4 + i], ACT.Sqrt).then_inc(S("rms"), 1)
            act.wait_ge(S("states_stored"), 160)

        def angles(eng, do, part):
            js = slice(part * NJ // 2, (part + 1) * NJ // 2)
            c, s, tmp = ct[:, js, :], sn[:, js, :], ttmp[part]
            do(eng.tensor_copy(c[:, :, 0], pcol[:, M_COS, js]))
            do(eng.tensor_copy(s[:, :, 0], pcol[:, M_SIN, js]))
            m = 1
            while m < TP:
                cm = c[:, :, m - 1:m].to_broadcast([P, NJ // 2, m])
                sm_ = s[:, :, m - 1:m].to_broadcast([P, NJ // 2, m])
                old, new = slice(0, m), slice(m, 2 * m)
                do.start(eng.tensor_tensor(c[:, :, new], c[:, :, old], cm, ALU.mult))
                do.start(eng.tensor_tensor(s[:, :, new], s[:, :, old], cm, ALU.mult))
                do(eng.tensor_tensor(tmp[:, :, 0:m], s[:, :, old], sm_, ALU.mult))
                do(eng.tensor_tensor(c[:, :, new], c[:, :, new], tmp[:, :, 0:m], ALU.subtract))
                do(eng.tensor_tensor(tmp[:, :, 0:m], c[:, :, old], sm_, ALU.mult))
                do(eng.tensor_tensor(s[:, :, new], s[:, :, new], tmp[:, :, 0:m], ALU.add))
                m *= 2
            do.start(eng.tensor_copy(c[:, :, TP:T], c[:, :, 0:TS]))
            do(eng.tensor_copy(s[:, :, TP:T], s[:, :, 0:TS]))

        @block.gpsimd
        def _(pool):
            do = Order(pool, "pool_order")
            nc.gpsimd.memset(wg, 0.0).then_inc(S("wg_zero"), 1)
            nc.gpsimd.memset(btz, 0.0).then_inc(S("btz_zero"), 1)
            nc.gpsimd.memset(bpad, 0.0).then_inc(S("btz_zero"), 1)
            pool.wait_ge(S("cnat_landed"), 32)
            pool.wait_ge(S("cst2_landed"), 16)
            for k in range(2):
                for par in range(2):
                    c = C_PAR - C_KEEP + par
                    do(nc.gpsimd.tensor_scalar(cpad[:, k, :, par, :], cnat[:, k], cst2[:, c:c + 1], None, ALU.mult))
            pool.sem_inc(S("cpad_ready"), 1)
            pool.wait_ge(S("pcol_ready"), 1)
            pool.wait_ge(S("xnT_ready"), 3)
            nc.gpsimd.memset(vn[:, :, :, HD:HD + 1], 1.0).then_inc(S("vn_ones"), 1)
            angles(nc.gpsimd, do, 1)
            pool.sem_inc(S("table_ready"), 1)

            def s5_in(j):
                b = j % 2
                C, Sn = ct[:, j, :], sn[:, j, :]
                if j == 0:
                    pool.wait_ge(S("table_ready"), 2)
                pool.wait_ge(S("g_ready"), j + 1)
                if j >= 2:
                    pool.wait_ge(S("y_done"), j - 1)
                tt = nc.gpsimd.tensor_tensor
                do.start(tt(ptmp[:, 0, :], Sn, zz[:, b, 1, :], ALU.mult))
                do.start(tt(hh[:, b, 0, :], C, zz[:, b, 0, :], ALU.mult))
                do.start(tt(ptmp[:, 1, :], Sn, zz[:, b, 0, :], ALU.mult))
                do(tt(hh[:, b, 1, :], C, zz[:, b, 1, :], ALU.mult))
                do(tt(hh[:, b, 0, :], hh[:, b, 0, :], ptmp[:, 0, :], ALU.subtract))
                tt(hh[:, b, 1, :], hh[:, b, 1, :], ptmp[:, 1, :], ALU.add).then_inc(S("h_ready"), 1)
                pool.wait_ge(S("h_ready"), j + 1)
                nc.gpsimd.tensor_copy(fin[:, 0:2, j], hh[:, b, :, TP - 1]).then_inc(S("fin_ready"), 1)
                nc.gpsimd.tensor_copy(fin[:, 2:4, j], hh[:, b, :, T - 1]).then_inc(S("fin_ready"), 1)

            def chunk(c):
                if c == 0:
                    pool.wait_ge(S("nat_read"), 2 * NC)
                    pool.wait_ge(S("vn_ones"), 1)
                    pool.wait_ge(S("cols_ready"), 1)
                    pool.wait_ge(S("y_done"), NJ)
                else:
                    pool.wait_ge(S("u_done"), c)
                nc.gpsimd.tensor_tensor(vw, vn[:, c], wcol[:, 1, c, :][:, :, None].to_broadcast([CH, H, HD + 1]),
                                        ALU.mult).then_inc(S("vw_ready"), 1)

            steps = dict(s5_in=s5_in, chunk=chunk)
            for j in range(T_ML):
                for step, n in plan[j]:
                    if step in steps:
                        steps[step](n)
            pool.wait_ge(S("cn_ready"), NC)
            pool.wait_ge(S("hT_read"), NC)
            pool.wait_ge(S("co_read"), 4)
            pool.wait_ge(S("mix_ready"), 8)
            for q in range(3):
                do(nc.gpsimd.memset(parts[64:128, q, 2, :], 0.0))
            pool.sem_inc(S("zeros_set"), 1)
            do(nc.gpsimd.memset(tab[:, :, :], 0.0))
            pool.sem_inc(S("zeros_set"), 1)
            pool.wait_ge(S("bdn_landed"), 48)
            do(nc.gpsimd.tensor_copy(bd3, bdn))
            for q in (1, 2):
                for part in range(1, q + 1):
                    r32 = slice(q * NE, (q + 1) * NE)
                    do(nc.gpsimd.tensor_tensor(bdn[r32], bdn[r32], bd3[r32], ALU.subtract))
                    do(nc.gpsimd.tensor_copy(bd3[r32], bdn[r32]))
            pool.sem_inc(S("parts_ready"), 1)
            for name, n in (("cur_set", 1), ("added", 2), ("gus_ready", 2), ("turned", 2), ("gathered", 1),
                            ("pt_done", 1), ("pool_pw", 3), ("chunks_used", CHUNKS)):
                pool.sem_inc(S(name), n)
            def first_rest(i):
                n = TILES[i][1]
                pool.wait_ge(S("hi_ready"), i + 1)
                nc.gpsimd.tensor_tensor(rest[0:n, i, :], xm[i][0:n, :], parts[0:n, 0, i, :], ALU.subtract).then_inc(S("rest"), 1)

            first_rest(0)
            for i, (t0, n) in enumerate(TILES):
                if i < 2:
                    first_rest(i + 1)
                pool.wait_ge(S("mid_ready"), i + 1)
                nc.gpsimd.tensor_tensor(parts[0:n, 2, i, :], rest[0:n, i, :], parts[0:n, 1, i, :], ALU.subtract).then_inc(S("parts_ready"), 1)
            pool.wait_ge(S("parts_ready"), 4)
            pool.wait_ge(S("group_used"), 28)
            do(nc.gpsimd.memset(pt, 0.0))
            pool.sem_inc(S("osb_ready"), 2)
            pool.sem_inc(S("pt_ready"), 1)
            pool.wait_ge(S("cum_ready"), 1)

            with pool.Fori(0, NE) as e:
                first = pool.value_load(cum[0:1, bass.ds(e, 1)], min_val=0, max_val=NE * MAXB)
                end = pool.value_load(cum[0:1, bass.ds(e + 1, 1)], min_val=1, max_val=NE * MAXB)
                pool.wait_ge(S("cur_set"), first + e + 1)
                pool.sem_inc(S("pool_go"), 1)
                nc.gpsimd.tensor_copy(cur[:, 0:3], tab[:, bass.ds(e, 1), 0:3].rearrange("p a b -> p (a b)")).then_inc(S("cur_set"), 1)
                with pool.Fori(first, end) as g:
                    ts = nc.gpsimd.tensor_scalar
                    pool.wait_ge(S("cur_set"), g + e + 2)
                    pool.wait_ge(S("gathered"), g + 1)
                    pool.sem_inc(S("pool_go"), 1)
                    for i in range(3):
                        ts(pb[:, i, :], cst[:, C_SLOT:C_SLOT + SLOT], cur[:, i:i + 1], None, ALU.is_equal).then_inc(S("pool_p"), 1)
                    pool.wait_ge(S("pool_p"), 3 * g + 3)
                    pool.sem_inc(S("p_ready"), 1)
                    pool.wait_ge(S("gates_tab"), 1)
                    pool.wait_ge(S("pool_pw"), 3 * g + 3)
                    pool.sem_inc(S("pool_go"), 1)
                    nc.gpsimd.tensor_copy(cur[:, 3:6], tab[:, bass.ds(e, 1), 3:6].rearrange("p a b -> p (a b)")).then_inc(S("gates_in"), 1)
                    pool.wait_ge(S("gates_in"), g + 1)
                    pool.wait_ge(S("pt_done"), g + 1)
                    pool.sem_inc(S("pool_go"), 1)
                    for i in range(3):
                        ts(pw[:, i, :], cst[:, C_SLOT:C_SLOT + P], cur[:, i:i + 1], cur[:, 3 + i:4 + i],
                           ALU.is_equal, ALU.mult).then_inc(S("pool_pw"), 1)
                    pool.wait_ge(S("pool_pw"), 3 * g + 6)
                    pool.sem_inc(S("pw_ready"), 1)
                    ts(cur[:, 0:3], cur[:, 0:3], float(SLOT), None, ALU.subtract).then_inc(S("cur_set"), 1)
            pool.sem_inc(S("p_ready"), 1)

        @block.vector
        def _(dve):
            v = nc.vector
            do = Order(dve, "dve_order")

            def inverse_rms(i, n, k):
                dve.wait_ge(S("ss"), 3 * k + i + 1)
                v.tensor_scalar(st[0:n, 3 + i:4 + i], st[0:n, i:i + 1], 1.0 / D, EPS, ALU.mult, ALU.add).then_inc(S("ms"), 1)
                dve.wait_ge(S("rms"), 3 * k + i + 1)
                do(v.reciprocal(st[0:n, 9 + i:10 + i], st[0:n, 6 + i:7 + i]))
                return st[0:n, 9 + i:10 + i]

            for i, (t0, n) in enumerate(TILES):
                inv = inverse_rms(i, n, 0)
                v.tensor_scalar(xn[0:n, i, :], acc[0:n, i, :], inv, None, ALU.mult).then_inc(S("xn_ready"), 1)
            dve.wait_ge(S("vcT"), 1)
            v.tensor_copy(vc[:, :], psum[:, 0, 0:16]).then_inc(S("vc_ready"), 1)
            dve.wait_ge(S("vc_ready"), 1)
            for i, (t0, n) in enumerate(TILES):
                dve.wait_ge(S("xT"), i + 1)
                src = cut(flat(psum[:, 2 + 2 * i:4 + 2 * i, :]), DK, P)[:, :, 0:n]
                v.tensor_tensor(xnT[:, :, t0:t0 + n], src, vc[:, 0:DK][:, :, None].to_broadcast([P, DK, n]),
                                ALU.mult).then_inc(S("xnT_ready"), 1)

            def q(k):
                return prm[:, k, :]
            dve.wait_ge(S("dt_ready"), 1)
            dt = prm[:, LDT, 2:4][:, :, None].to_broadcast([NJ, 2, S5P])
            v.tensor_tensor(cut(q(X0), 2, S5P), cut(q(A_RE), 2, S5P), dt, ALU.mult).then_inc(S("dar"), 1)
            do(v.tensor_tensor(cut(q(DAI), 2, S5P), cut(q(A_IM), 2, S5P), dt, ALU.mult))
            do(v.tensor_scalar(q(X1), q(DAI), 1.0 / TWO_PI, ROUND, ALU.mult, ALU.add))
            do(v.tensor_scalar(q(X1), q(X1), ROUND, None, ALU.subtract))
            do(v.scalar_tensor_tensor(out=q(RED), in0=q(X1), scalar=-PI2_A, in1=q(DAI), op0=ALU.mult, op1=ALU.add))
            do(v.scalar_tensor_tensor(out=q(RED), in0=q(X1), scalar=-PI2_B, in1=q(RED), op0=ALU.mult, op1=ALU.add))
            do(v.scalar_tensor_tensor(out=q(RED), in0=q(X1), scalar=-PI2_C, in1=q(RED), op0=ALU.mult, op1=ALU.add))
            do(v.tensor_scalar(q(RED), q(RED), PI_IN, -PI_IN, ALU.min, ALU.max))
            do(v.scalar_tensor_tensor(out=q(X2), in0=q(RED), scalar=-1.0, in1=q(RED), op0=ALU.mult, op1=ALU.min))
            do(v.tensor_scalar(q(X2), q(X2), TWO_PI / 4, None, ALU.add))
            dve.sem_inc(S("reduced"), 1)
            dve.wait_ge(S("sincos"), 3)
            do(v.tensor_tensor(q(X0), q(MAG), q(COS), ALU.mult))
            do(v.tensor_tensor(q(X1), q(MAG), q(SIN), ALU.mult))
            do(v.tensor_tensor(q(DEN), q(A_RE), q(A_RE), ALU.mult))
            do(v.tensor_tensor(q(X2), q(A_IM), q(A_IM), ALU.mult))
            do(v.tensor_tensor(q(DEN), q(DEN), q(X2), ALU.add))
            do(v.reciprocal(q(DEN), q(DEN)))
            do(v.tensor_scalar(q(X0), q(X0), 1.0, None, ALU.subtract))
            do(v.tensor_tensor(q(FR), q(X0), q(A_RE), ALU.mult))
            do(v.tensor_tensor(q(X2), q(X1), q(A_IM), ALU.mult))
            do(v.tensor_tensor(q(FR), q(FR), q(X2), ALU.add))
            do(v.tensor_tensor(q(FR), q(FR), q(DEN), ALU.mult))
            do(v.tensor_tensor(q(FI), q(X1), q(A_RE), ALU.mult))
            do(v.tensor_tensor(q(X2), q(X0), q(A_IM), ALU.mult))
            do(v.tensor_tensor(q(FI), q(FI), q(X2), ALU.subtract))
            do(v.tensor_tensor(q(FI), q(FI), q(DEN), ALU.mult))
            dve.sem_inc(S("prm_ready"), 1)

            def s5_columns(_):
                dve.wait_ge(S("prmT"), 1)
                v.tensor_copy(flat(pcol), psum[:, 2, 0:7 * NJ]).then_inc(S("pcol_ready"), 1)
                dve.wait_ge(S("pcol_ready"), 1)
                dve.wait_ge(S("bnat_landed"), 32)
                dve.wait_ge(S("btz_zero"), 2)
                fr = pcol[:, M_FR, :][:, :, None].to_broadcast([P, NJ, S5C])
                fi = pcol[:, M_FI, :][:, :, None].to_broadcast([P, NJ, S5C])
                for n, (f, k) in enumerate(((fr, 0), (fi, 1), (fr, 1), (fi, 0))):
                    do(v.tensor_tensor(btmp2[:, n], bnat[:, k], f, ALU.mult))
                for par in range(2):
                    s, c = slice(64 * par, 64 * par + 64), slice(S5C * par, S5C * par + S5C)
                    do(v.tensor_tensor(bpad[s, 0, :, c], btmp2[s, 0], btmp2[s, 1], ALU.subtract))
                    do(v.tensor_tensor(bpad[s, 1, :, c], btmp2[s, 2], btmp2[s, 3], ALU.add))
                dve.sem_inc(S("bpad_ready"), 1)

            def tables(_):
                angles(v, do, 0)
                dve.sem_inc(S("table_ready"), 1)

            def gate_rows(_):
                dve.wait_ge(S("gate_rows"), 1)
                R = rows
                v.scalar_tensor_tensor(out=R[R_B], in0=R[R_LF], scalar=-1.0, in1=R[R_LF], op0=ALU.mult, op1=ALU.max).then_inc(S("fabs"), 1)
                dve.wait_ge(S("softplus"), 1)
                do(v.scalar_tensor_tensor(out=R[R_LF], in0=R[R_LF], scalar=0.0, in1=R[R_AL], op0=ALU.min, op1=ALU.subtract))
                seg = cst2[0:H, C_SEG - C_KEEP:C_SEG - C_KEEP + T]
                do(v.tensor_tensor_scan(R[R_B], seg, R[R_LF], 0.0, ALU.mult, ALU.add))
                do(v.tensor_tensor_scan(R[R_M][:, 0:TP], R[R_LF][:, 0:TP], R[R_IG][:, 0:TP], 0.0, ALU.add, ALU.max))
                do(v.tensor_tensor_scan(R[R_M][:, TP:T], R[R_LF][:, TP:T], R[R_IG][:, TP:T], bcol[0:H, 1:2], ALU.add, ALU.max))
                do(v.tensor_tensor(R[R_A], R[R_IG], R[R_B], ALU.subtract))
                do(v.tensor_tensor(R[R_AL], R[R_B], R[R_M], ALU.subtract))
                al, wi, m = by_chunk(R_AL), by_chunk(R_WI), by_chunk(R_M)
                do(v.tensor_copy(wi[:, 0, :], al[:, 0, :]))
                do(v.tensor_tensor(wi[:, 1:NCP, :], al[:, 1:NCP, :], m[:, 0:NCP - 1, CH - 1:CH].to_broadcast([H, NCP - 1, CH]), ALU.add))
                do(v.tensor_scalar(wi[:, NCP, :], al[:, NCP, :], bcol[0:H, 1:2], None, ALU.add))
                do(v.tensor_tensor(by_chunk(R_WE), by_chunk(R_A), al[:, :, CH - 1:CH].to_broadcast([H, NC, CH]), ALU.add))
                dve.sem_inc(S("wexp"), 1)

            def state_in(_):
                pass

            def decay_matrix(h):
                dve.wait_ge(S("dm_done"), h + 1)
                mask = cst2[0:CH, C_CAUSAL - C_KEEP:C_CAUSAL - C_KEEP + CH][:, None, :].to_broadcast([CH, NC, CH])
                v.tensor_tensor(wt[:, h], cut(psum[0:CH, 6 + h % 2, 0:T], NC, CH), mask, ALU.add).then_inc(S("dm_read"), 1)

            def s5_in(j):
                b = j % 2
                C, Sn, br, bi = ct[:, j, :], sn[:, j, :], psum[:, 2, 0:T], psum[:, 3, 0:T]
                if j == 0:
                    dve.wait_ge(S("table_ready"), 2)
                dve.wait_ge(S("bu_done"), j + 1)
                if j >= 2:
                    dve.wait_ge(S("h_ready"), j - 1)
                do.start(v.tensor_tensor(dtmp[:, 0, :], Sn, bi, ALU.mult))
                do.start(v.tensor_tensor(zz[:, b, 0, :], C, br, ALU.mult))
                do.start(v.tensor_tensor(dtmp[:, 1, :], Sn, br, ALU.mult))
                v.tensor_tensor(zz[:, b, 1, :], C, bi, ALU.mult).then_inc(S("bu_read"), 1)
                do.wait()
                do.start(v.tensor_tensor(zz[:, b, 0, :], zz[:, b, 0, :], dtmp[:, 0, :], ALU.add))
                dve.wait_ge(S("bu_read"), j + 1)
                do(v.tensor_tensor(zz[:, b, 1, :], zz[:, b, 1, :], dtmp[:, 1, :], ALU.subtract))
                for k in range(2):
                    mag = pcol[:, M_MAG, j:j + 1]
                    zp, zs = zz[:, b, k, 0:TP], zz[:, b, k, TP:T]
                    do.start(v.tensor_tensor_scan(zp, mag.to_broadcast([P, TP]), zp, 0.0, ALU.mult, ALU.add))
                    do.start(v.tensor_tensor_scan(zs, mag.to_broadcast([P, TS]), zs, pcol[:, M_H0R + k, j:j + 1], ALU.mult, ALU.add))
                do.wait()
                dve.sem_inc(S("g_ready"), 1)

            def s5_out(j):
                t = j // 4
                if j % 4 == 3:
                    dve.wait_ge(S("y_done"), j + 1)
                    do(v.scalar_tensor_tensor(out=uT[:, t, :], in0=uT[:, t, :], scalar=vc[:, 8 + t:9 + t], in1=psum[:, 4, 0:T],
                                              op0=ALU.mult, op1=ALU.add))
                    dve.sem_inc(S("y_read"), 1)

            def scores(h):
                dve.wait_ge(S("sc_done"), h + 1)
                dve.wait_ge(S("wt_ready"), h + 1)
                v.tensor_tensor(flat(wt[:, h]), psum[0:CH, 6 + h % 2, 0:T], flat(wt[:, h]), ALU.mult).then_inc(S("st_ready"), 1)

            def pairs(ap):
                return ap.rearrange("p (b h) v -> p b h v", b=2)

            def banks(b, n):
                return psum[0:n, b:b + 2, 0:2 * (HD + 1)].rearrange("p b (h v) -> p b h v", h=2)

            def chunk(c):
                dve.wait_ge(S("u_done"), c + 1)
                new = cn[:, (c + 1) % 2]
                if c == 0:
                    do(v.tensor_copy(pairs(new), banks(6, P)))
                else:
                    old = cn[:, c % 2] if c < NCP else cn0
                    for h in range(H):
                        do.start(v.scalar_tensor_tensor(out=new[:, h, :], in0=old[:, h, :], scalar=dec[:, h, c:c + 1],
                                                        in1=psum[:, 6 + h // 2, (h % 2) * 129:(h % 2) * 129 + 129],
                                                        op0=ALU.mult, op1=ALU.add))
                    do.wait()
                dve.sem_inc(S("cn_ready"), 1)
                dve.wait_ge(S("a_done"), c + 1)
                if c == 0:
                    dve.wait_ge(S("h_ready"), NJ)
                    dve.wait_ge(S("y_done"), NJ)
                    do(v.tensor_copy(pairs(num), banks(2, CH)))
                else:
                    dve.wait_ge(S("b_done"), c)
                    wi = pairs(wcol[:, 0, c, :][:, :, None].to_broadcast([CH, H, HD + 1]))
                    do(v.tensor_tensor(pairs(num), banks(4, CH), wi, ALU.mult))
                    do(v.tensor_tensor(pairs(num), pairs(num), banks(2, CH), ALU.add))
                dve.sem_inc(S("num_read"), 1)
                d4 = den[0:CH, 0:H]
                do(v.scalar_tensor_tensor(out=d4, in0=num[:, :, HD], scalar=-1.0, in1=num[:, :, HD], op0=ALU.mult, op1=ALU.max))
                do(v.tensor_tensor(d4, d4, wcol[:, 2, c, :], ALU.max))
                do(v.reciprocal(d4, d4))
                if c > 0:
                    dve.wait_ge(S("hT_done"), c)
                do(v.tensor_tensor(hn, num[:, :, 0:HD], d4[:, :, None].to_broadcast([CH, H, HD]), ALU.mult))
                for h in range(H):
                    do.start(v.bn_stats(bns[0:CH, h, :], hn[:, h, :]))
                do.wait()
                for h in range(H):
                    do.start(v.bn_aggr(mv[0:CH, h, :], bns[0:CH, h, :]))
                do.wait()
                v.tensor_scalar(d4, mv[0:CH, :, 1], EPS, None, ALU.add).then_inc(S("var_ready"), 1)
                dve.wait_ge(S("std_ready"), c + 1)
                s4 = den[0:CH, H:2 * H]
                do(v.reciprocal(s4, s4))
                for h in range(H):
                    do.start(v.tensor_scalar(hn[:, h, :], hn[:, h, :], mv[0:CH, h, 0:1], s4[:, h:h + 1], ALU.subtract, ALU.mult))
                do.wait()
                dve.sem_inc(S("hn_ready"), 1)

            def turn(c):
                dve.wait_ge(S("hT_done"), c + 1)
                for h in range(H):
                    o = oT[:, h, c * CH:(c + 1) * CH]
                    do.start(v.scalar_tensor_tensor(out=o, in0=psum[:, 2, h * CH:(h + 1) * CH], scalar=vc[:, 12 + h:13 + h],
                                                    in1=o, op0=ALU.mult, op1=ALU.mult))
                do.wait()
                dve.sem_inc(S("hT_read"), 1)

            steps = dict(s5_columns=s5_columns, gate_rows=gate_rows, tables=tables, decay_matrix=decay_matrix,
                         s5_in=s5_in, s5_out=s5_out, scores=scores, chunk=chunk, turn=turn)

            def glu(p):
                j = T_GLU + 2 * p
                if p == 0:
                    dve.wait_ge(S("gates_ready"), 1)
                dve.wait_ge(S("pj_done"), j + 1)
                dve.wait_ge(S("pj_free1"), j // 2 + 1)
                sg_ = gtmp[p % 2]
                v.tensor_tensor(sg_, bank(j)[:, 0:T], sg_, ALU.mult).then_inc(S("pj_free0"), 1)
                dve.wait_ge(S("pj_free0"), j // 2 + 1)
                v.tensor_tensor(gS[:, p, :], gS[:, p, :], sg_, ALU.mult).then_inc(S("glu_done"), 1)

            for j in range(T_ML):
                for step, n in plan[j]:
                    if step in steps:
                        steps[step](n)
                if j >= T_GLU and j % 2 == 1:
                    glu((j - T_GLU) // 2)
            dve.wait_ge(S("glu_done"), 8)
            for i in range(DK):
                j = T_ML + i
                dve.wait_ge(S("pj_done"), j + 1)
                if i > 1:
                    dve.wait_ge(S("mix_ready"), i - 1)
                v.tensor_tensor(gtmp[i % 2], bank(j)[:, 0:T], gM[:, i, :], ALU.mult).then_inc(S(f"pj_free{j % 2}"), 1)
                dve.wait_ge(S(f"pj_free{j % 2}"), j // 2 + 1)
                v.tensor_tensor(gS[:, i, :], gS[:, i, :], gtmp[i % 2], ALU.add).then_inc(S("mix_ready"), 1)
            dve.wait_ge(S("res_landed"), 64)

            def turned_rows(i):
                t0, n = TILES[i]
                dve.wait_ge(S("xmT"), i + 1)
                src = cut(flat(psum[:, XT[i]:XT[i] + 2, :]), DK, P)[:, :, 0:n]
                v.tensor_copy(xnT[:, :, t0:t0 + n], src).then_inc(S("xmT_ready"), 1)

            def residual(gg, i):
                n = TILES[i][1]
                j = T_OUT + 3 * gg + i
                dve.wait_ge(S("pj_done"), j + 1)
                x = acc[0:n, i, 256 * gg:256 * gg + 256]
                v.tensor_tensor(x, x, bank(j)[0:n, 0:256], ALU.add).then_inc(S(f"pj_free{j % 2}"), 1)
                dve.wait_ge(S(f"pj_free{j % 2}"), j // 2 + 1)

            for gg in range(3):
                for i in range(3):
                    residual(gg, i)
            for i, (t0, n) in enumerate(TILES):
                residual(3, i)
                dve.sem_inc(S("x1_ready"), 1)
                if i == 2:
                    turned_rows(0)
                inv = inverse_rms(i, n, 1)
                if i == 2:
                    dve.wait_ge(S("group_used"), 28)
                v.scalar_tensor_tensor(out=xm[i][0:n, :], in0=acc[0:n, i, :], scalar=inv, in1=nmb[0:n, :],
                                       op0=ALU.mult, op1=ALU.mult).then_inc(S("xm_ready"), 1)
            turned_rows(1)
            turned_rows(2)
            exps = cst[:, C_EXP:C_EXP + NE]
            do(v.memset(cumf[:, 2, 0:1], 0.0))
            dve.wait_ge(S("wrt_landed"), 32)
            def of(i):
                n = TILES[i][1]
                return [n] + [x[0:n] for x in top[i]]

            for group in ((0,), (1, 2)):
                for i in group:
                    n, lg, t8, i8, f8 = of(i)
                    dve.wait_ge(S("logits"), i + 1)
                    do.start(v.tensor_tensor(lg, psum[0:n, i, 0:NE], brt[0:n, :], ALU.add))
                do.wait()
                for i in group:
                    n, lg, t8, i8, f8 = of(i)
                    do.start(v.max(t8, lg))
                do.wait()
                for i in group:
                    n, lg, t8, i8, f8 = of(i)
                    do.start(v.max_index(i8, t8, lg))
                do.wait()
                for i in group:
                    n, lg, t8, i8, f8 = of(i)
                    do.start(v.tensor_copy(f8[:, 0:TOPK], i8[:, 0:TOPK]))
                do.wait()
                for k in range(TOPK):
                    for i in group:
                        n, lg, t8, i8, f8 = of(i)
                        m = msk[0:n, i, :]
                        if k == 0:
                            do.start(v.tensor_scalar(m, exps[0:n, :], f8[:, 0:1], None, ALU.is_equal))
                        else:
                            do.start(v.scalar_tensor_tensor(out=m, in0=exps[0:n, :], scalar=f8[:, k:k + 1], in1=m,
                                                            op0=ALU.is_equal, op1=ALU.add))
                    do.wait()
                dve.sem_inc(S("mask_ready"), len(group))
                for i in group:
                    n, lg, t8, i8, f8 = of(i)
                    v.tensor_scalar(f8[:, 8:9], t8[:, 0:1], -1.0, None, ALU.mult).then_inc(S("top_ready"), 1)
            dve.wait_ge(S("ranks"), 1)
            dve.wait_ge(S("zeros_set"), 2)
            for i, (t0, n) in enumerate(TILES):
                do.start(v.scalar_tensor_tensor(out=tab[0:n, :, i], in0=psum[0:n, 4, i * NE:(i + 1) * NE], scalar=1.0, in1=msk[0:n, i, :],
                                                op0=ALU.add, op1=ALU.mult))
            cnt = psum[0:1, 3, 0:NE]
            do(v.tensor_scalar(cumf[:, 0, 1:], cnt, float(SLOT), 1.0, ALU.is_gt, ALU.add))
            for b in range(2, MAXB):
                do(v.scalar_tensor_tensor(out=cumf[:, (b - 1) % 2, 1:], in0=cnt, scalar=float(b * SLOT), in1=cumf[:, b % 2, 1:],
                                          op0=ALU.is_gt, op1=ALU.add))
            do(v.tensor_tensor_scan(cumf[:, 2, 1:], ones[0:1, 0:NE], cumf[:, (MAXB - 2) % 2, 1:], 0.0, ALU.mult, ALU.add))
            do(v.tensor_copy(cum[:, :], cumf[:, 2, :]))
            dve.sem_inc(S("cum_ready"), 1)
            for i, (t0, n) in enumerate(TILES):
                lg, t8, i8, f8 = (x[0:n] for x in top[i])
                dve.wait_ge(S("top_exp"), i + 1)
                do(v.reciprocal(f8[:, 10:11], f8[:, 9:10]))
                do(v.tensor_scalar(f8[:, 11:15], f8[:, 4:8], f8[:, 10:11], None, ALU.mult))
                for k in range(TOPK):
                    dst = tk[0:n, :] if k else lg
                    do(v.tensor_scalar(dst, exps[0:n, :], f8[:, k:k + 1], f8[:, 11 + k:12 + k], ALU.is_equal, ALU.mult))
                    if k:
                        do(v.tensor_tensor(lg if k < TOPK - 1 else tab[0:n, :, 3 + i], lg, tk[0:n, :], ALU.add))
            dve.sem_inc(S("gates_tab"), 1)

            def x_columns(g):
                dve.wait_ge(S("gathered"), g + 2)
                v.tensor_copy(flat(xeT), psum[:, XB, :]).then_inc(S("xe_ready"), 1)

            def add(g, k):
                i, hf = k // 2, k % 2
                n = TILES[i][1]
                dve.wait_ge(S("combined"), 6 * g + (k + 1))
                x = acc[0:n, i, hf * 512:(hf + 1) * 512]
                v.tensor_tensor(x, x, psum[0:n, CB + hf, :], ALU.add).then_inc(S("added"), 1)

            x_columns(0)
            with dve.Fori(0, NE) as e:
                first = dve.value_load(cum[0:1, bass.ds(e, 1)], min_val=0, max_val=NE * MAXB)
                end = dve.value_load(cum[0:1, bass.ds(e + 1, 1)], min_val=1, max_val=NE * MAXB)
                with dve.Fori(first, end) as g:
                    for k in range(6):
                        add(g, k)
                    bias = bg[:, bass.ds(e, 1), :, :].rearrange("p o g m -> p (o m) g")
                    for hf in range(2):
                        m4 = slice(4 * hf, 4 * hf + 4)
                        dve.wait_ge(S("turned"), 2 * g + (hf + 3))
                        v.tensor_tensor(hb[:, m4], cut(psum[:, DN + hf, :], 4, 2, SLOT),
                                        bias[:, m4, :, None].to_broadcast([P, 4, 2, SLOT]), ALU.add).then_inc(S("biased"), 1)
                        dve.wait_ge(S("biased"), 2 * g + (hf + 1))
                        v.tensor_scalar(hb[:, m4, 0, :], hb[:, m4, 0, :], LIMIT, None, ALU.min).then_inc(S("clamped"), 1)
                        v.tensor_scalar(hb[:, m4, 1, :], hb[:, m4, 1, :], LIMIT, -LIMIT, ALU.min, ALU.max).then_inc(S("up_clamped"), 1)
                    for hf in range(2):
                        m4 = slice(4 * hf, 4 * hf + 4)
                        dve.wait_ge(S("sg_ready"), 2 * g + (hf + 1))
                        v.tensor_tensor(sg[:, m4], hb[:, m4, 0, :], sg[:, m4], ALU.mult).then_inc(S("swished"), 1)
                        dve.wait_ge(S("swished"), 2 * g + (hf + 1))
                        dve.wait_ge(S("up_clamped"), 2 * g + (hf + 1))
                        v.scalar_tensor_tensor(out=hT[:, m4], in0=hb[:, m4, 1, :], scalar=1.0, in1=sg[:, m4],
                                               op0=ALU.add, op1=ALU.mult).then_inc(S("hT_ready"), 1)
                    x_columns(g + 1)
                    dve.wait_ge(S("pt_done"), g + 2)
                    v.tensor_copy(pt, psum[:, PTB, 0:T]).then_inc(S("pt_ready"), 1)
            blocks = dve.value_load(cum[0:1, NE:NE + 1], min_val=1, max_val=NE * MAXB)
            dve.wait_ge(S("nfb_landed"), 16)

            def last_adds(i):
                add(blocks, 2 * i)
                add(blocks, 2 * i + 1)
                dve.wait_ge(S("added"), 6 * blocks + (2 * i + 4))
                dve.sem_inc(S("acc_ready"), 1)

            last_adds(0)
            last_adds(1)
            for i, (t0, n) in enumerate(TILES):
                if i == 1:
                    last_adds(2)
                inv = inverse_rms(i, n, 2)
                v.scalar_tensor_tensor(out=acc[0:n, i, :], in0=acc[0:n, i, :], scalar=inv, in1=nfb[0:n, :],
                                       op0=ALU.mult, op1=ALU.mult).then_inc(S("y_ready"), 1)


_INS = ["x_prompt", "x_sample", "state_s5_re", "state_s5_im", "state_ml_C", "state_ml_n", "state_ml_m",
        "norm_mix", "w_in", "b_ig", "b_fg", "s5_a_re", "s5_a_im", "s5_log_dt", "s5_b_re", "s5_b_im",
        "s5_c_re", "s5_c_im", "s5_d", "w_s5_glu", "ml_gn", "w_ml_out", "w_out", "norm_moe", "w_router",
        "b_router", "w_gate_up", "b_gate_up", "w_down", "b_down", "norm_final"]
_STATES = [(1, 1, S5G, S5P), (1, 1, S5G, S5P), (1, 1, H, HD, HD), (1, 1, H, HD), (1, 1, H)]
_OUTS = [(1, TP, D), (1, TS, D)] + _STATES + _STATES


def kernel(**inputs):
    import numpy as _np
    import concourse.bacc as _bacc
    from concourse import mybir as _mybir
    from concourse.bass_utils import run_bass_kernel_spmd as _run

    nc = _bacc.Bacc("TRN2", target_bir_lowering=False, num_devices=1)
    arrays, args = {}, {}
    for name in _INS + ["consts"]:
        x = shape_constants() if name == "consts" else _np.ascontiguousarray(inputs[name])
        arrays[f"in_{name}_dram"] = x
        args[name] = nc.dram_tensor(f"in_{name}_dram", x.shape, _mybir.dt.from_np(x.dtype), kind="ExternalInput").ap()
    outs = [nc.dram_tensor(f"out_{i}_dram", s, F32, kind="ExternalOutput").ap() for i, s in enumerate(_OUTS)]
    hybrid_stream_step(nc, args, outs)
    r = _run(nc, [arrays], core_ids=[0])
    return tuple(r.results[0][f"out_{i}_dram"] for i in range(len(_OUTS)))
```
